# Optimizing a Trainium2 kernel written in Bass

```python
import jax, jax.numpy as jnp
from jax import lax
import numpy as np

D_MODEL = 1024
BATCH = 1
SEQ = 1024
DEPTH = 2

N_TOKEN_MIXERS = 2
N_MLSTM_LAYERS = (DEPTH + N_TOKEN_MIXERS - 1) // N_TOKEN_MIXERS
N_POOL_LAYERS = DEPTH // N_TOKEN_MIXERS
EXPAND = 2
E_A = EXPAND * D_MODEL
N_HEADS_A = 8
DV_A = E_A // N_HEADS_A
DK_A = DV_A // 2
CONV_K = 4
CHUNK = 128
A_IN_COLS = 3 * E_A + 2 * N_HEADS_A
E_B = EXPAND * D_MODEL
POOL_WINDOWS = (2, 4, 8, 16)
N_GROUPS_B = len(POOL_WINDOWS)
CG_B = E_B // N_GROUPS_B
B_IN_COLS = 2 * E_B
LN_EPS = 1e-5
DEEPNORM_ALPHA = (2.0 * DEPTH) ** 0.25
DEEPNORM_BETA = (8.0 * DEPTH) ** -0.25

kernel_name = "hybrid_mlstm_multiscale_pool_deepnorm"

def _layer_norm(x, g, b):
    xf = x.astype(jnp.float32)
    mu = xf.mean(-1, keepdims=True)
    var = jnp.square(xf - mu).mean(-1, keepdims=True)
    y = (xf - mu) * lax.rsqrt(var + LN_EPS) * g.astype(jnp.float32) + b.astype(jnp.float32)
    return y.astype(x.dtype)

def _causal_dwconv(u, w, b):
    y = lax.conv_general_dilated(
        u, w[:, None, :], window_strides=(1,), padding=[(CONV_K - 1, 0)],
        dimension_numbers=("NWC", "WIO", "NWC"), feature_group_count=u.shape[-1])
    return y + b

def _mlstm_chunkwise(q, k, v, log_i, log_f):
    B, S, H, DK = q.shape
    DV = v.shape[-1]
    NC = S // CHUNK

    def to_chunks(a):
        a = a.reshape((B, NC, CHUNK, H) + a.shape[3:])
        return jnp.moveaxis(jnp.moveaxis(a, 1, 0), 3, 2)

    qc, kc, vc = to_chunks(q), to_chunks(k), to_chunks(v)
    lic, lfc = to_chunks(log_i), to_chunks(log_f)
    causal = jnp.tril(jnp.ones((CHUNK, CHUNK), dtype=bool))

    def step(carry, inp):
        C, n, m = carry
        qq, kk, vv, li, lf = inp
        bcum = jnp.cumsum(lf, axis=-1)
        g = bcum + m[..., None]
        D = bcum[..., :, None] - bcum[..., None, :] + li[..., None, :]
        D = jnp.where(causal, D, -jnp.inf)
        m_t = jnp.maximum(g, D.max(-1))
        w_intra = jnp.exp(D - m_t[..., None])
        w_inter = jnp.exp(g - m_t)
        s = jnp.einsum("bhtd,bhsd->bhts", qq, kk) * w_intra
        num = (jnp.einsum("bhts,bhsv->bhtv", s, vv)
               + w_inter[..., None] * jnp.einsum("bhtd,bhdv->bhtv", qq, C))
        den = s.sum(-1) + w_inter * jnp.einsum("bhtd,bhd->bht", qq, n)
        h = num / jnp.maximum(jnp.abs(den), jnp.exp(-m_t))[..., None]
        bL = bcum[..., -1]
        a = bL[..., None] - bcum + li
        m_new = jnp.maximum(bL + m, a.max(-1))
        w_c = jnp.exp(bL + m - m_new)
        w_s = jnp.exp(a - m_new[..., None])
        C_new = w_c[..., None, None] * C + jnp.einsum("bhs,bhsd,bhsv->bhdv", w_s, kk, vv)
        n_new = w_c[..., None] * n + jnp.einsum("bhs,bhsd->bhd", w_s, kk)
        return (C_new, n_new, m_new), h

    init = (jnp.zeros((B, H, DK, DV), jnp.float32),
            jnp.zeros((B, H, DK), jnp.float32),
            jnp.zeros((B, H), jnp.float32))
    _, hc = lax.scan(step, init, (qc, kc, vc, lic, lfc))
    return jnp.moveaxis(hc, 2, 3).transpose(1, 0, 2, 3, 4).reshape(B, S, H, DV)

def _mlstm_branch(x, w_in, conv_w, conv_b, w_q, w_k, w_v, b_i, b_f, norm_g, skip, w_out):
    B, S, _ = x.shape
    H = N_HEADS_A
    proj = x @ w_in
    xm = proj[..., :E_A]
    z = proj[..., E_A:2 * E_A]
    o_pre = proj[..., 2 * E_A:3 * E_A]
    i_pre = (proj[..., 3 * E_A:3 * E_A + H] + b_i).astype(jnp.float32)
    f_pre = (proj[..., 3 * E_A + H:] + b_f).astype(jnp.float32)
    xc = jax.nn.silu(_causal_dwconv(xm, conv_w, conv_b))
    xch = xc.reshape(B, S, H, DV_A)
    xmh = xm.reshape(B, S, H, DV_A)
    q = jnp.einsum("bshc,hcd->bshd", xch, w_q).astype(jnp.float32) * (DK_A ** -0.5)
    k = jnp.einsum("bshc,hcd->bshd", xch, w_k).astype(jnp.float32)
    v = jnp.einsum("bshc,hcv->bshv", xmh, w_v).astype(jnp.float32)
    h = _mlstm_chunkwise(q, k, v, i_pre, jax.nn.log_sigmoid(f_pre))
    mu = h.mean(-1, keepdims=True)
    var = jnp.square(h - mu).mean(-1, keepdims=True)
    hn = ((h - mu) * lax.rsqrt(var + LN_EPS)).reshape(B, S, E_A) * norm_g.astype(jnp.float32)
    hb = (jax.nn.sigmoid(o_pre.astype(jnp.float32)) * hn).astype(x.dtype) + skip * xc
    return (hb * jax.nn.silu(z)) @ w_out

def _pool_branch(x, w_in, w_group, scale, w_out):
    B, S, _ = x.shape
    proj = x @ w_in
    u = proj[..., :E_B]
    z = proj[..., E_B:]
    uf = u.astype(jnp.float32)
    csum = jnp.cumsum(uf, axis=1)
    pos = jnp.arange(S)
    means = []
    for gi, win in enumerate(POOL_WINDOWS):
        cg = csum[..., gi * CG_B:(gi + 1) * CG_B]
        prev = jnp.pad(cg, ((0, 0), (win, 0), (0, 0)))[:, :S]
        cnt = jnp.minimum(pos + 1, win).astype(jnp.float32)[None, :, None]
        means.append((cg - prev) / cnt)
    pooled = (jnp.concatenate(means, axis=-1) - uf).astype(x.dtype)
    pooled = pooled.reshape(B, S, N_GROUPS_B, CG_B)
    mixed = jnp.einsum("bsgc,gcd->bsgd", pooled, w_group).reshape(B, S, E_B) * scale
    return (mixed * jax.nn.silu(z)) @ w_out

def setup_inputs(seed: int = 0) -> dict:
    key = jax.random.key(seed)
    ks = jax.random.split(key, 20)
    NA, NB, H = N_MLSTM_LAYERS, N_POOL_LAYERS, N_HEADS_A
    nrm = lambda k, shape, s: jax.random.normal(k, shape, jnp.float32) * s
    f_bias = jnp.broadcast_to(jnp.linspace(3.0, 6.0, H, dtype=jnp.float32), (NA, H))
    return {
        "x": nrm(ks[0], (BATCH, SEQ, D_MODEL), 1.0),
        "mlstm_w_in": nrm(ks[1], (NA, D_MODEL, A_IN_COLS), D_MODEL ** -0.5),
        "mlstm_conv_w": nrm(ks[2], (NA, CONV_K, E_A), CONV_K ** -0.5),
        "mlstm_conv_b": nrm(ks[3], (NA, E_A), 0.01),
        "mlstm_w_q": nrm(ks[4], (NA, H, DV_A, DK_A), DV_A ** -0.5),
        "mlstm_w_k": nrm(ks[5], (NA, H, DV_A, DK_A), DV_A ** -0.5),
        "mlstm_w_v": nrm(ks[6], (NA, H, DV_A, DV_A), DV_A ** -0.5),
        "mlstm_b_i": nrm(ks[7], (NA, H), 0.1),
        "mlstm_b_f": f_bias + nrm(ks[8], (NA, H), 0.1),
        "mlstm_norm_g": 1.0 + nrm(ks[9], (NA, E_A), 0.02),
        "mlstm_skip": 1.0 + nrm(ks[10], (NA, E_A), 0.02),
        "mlstm_w_out": nrm(ks[11], (NA, E_A, D_MODEL), (E_A ** -0.5) * DEEPNORM_BETA),
        "pool_w_in": nrm(ks[12], (NB, D_MODEL, B_IN_COLS), D_MODEL ** -0.5),
        "pool_w_group": nrm(ks[13], (NB, N_GROUPS_B, CG_B, CG_B), CG_B ** -0.5),
        "pool_scale": 1.0 + nrm(ks[14], (NB, E_B), 0.02),
        "pool_w_out": nrm(ks[15], (NB, E_B, D_MODEL), (E_B ** -0.5) * DEEPNORM_BETA),
        "post_ln_g": 1.0 + nrm(ks[16], (DEPTH, D_MODEL), 0.02),
        "post_ln_b": nrm(ks[17], (DEPTH, D_MODEL), 0.02),
    }

def reference(x, mlstm_w_in, mlstm_conv_w, mlstm_conv_b, mlstm_w_q, mlstm_w_k, mlstm_w_v,
              mlstm_b_i, mlstm_b_f, mlstm_norm_g, mlstm_skip, mlstm_w_out,
              pool_w_in, pool_w_group, pool_scale, pool_w_out, post_ln_g, post_ln_b):
    for i in range(DEPTH):
        j = i // N_TOKEN_MIXERS
        if i % N_TOKEN_MIXERS == 0:
            branch = _mlstm_branch(x, mlstm_w_in[j], mlstm_conv_w[j], mlstm_conv_b[j],
                                   mlstm_w_q[j], mlstm_w_k[j], mlstm_w_v[j],
                                   mlstm_b_i[j], mlstm_b_f[j], mlstm_norm_g[j],
                                   mlstm_skip[j], mlstm_w_out[j])
        else:
            branch = _pool_branch(x, pool_w_in[j], pool_w_group[j], pool_scale[j], pool_w_out[j])
        x = _layer_norm(DEEPNORM_ALPHA * x + branch, post_ln_g[i], post_ln_b[i])
    return x


_drawn_inputs = setup_inputs


def setup_inputs(seed=0):
    import zlib

    import numpy as np

    out = dict(_drawn_inputs(seed))
    spreads = {}
    factors = {'mlstm_conv_b': 8.0,
     'mlstm_b_i': 64.0,
     'mlstm_norm_g': 31.357,
     'mlstm_skip': 29.076,
     'pool_scale': 27.288}
    for name, (base, spread) in spreads.items():
        noise = np.random.default_rng([zlib.crc32(name.encode()), seed]).standard_normal(out[name].shape)
        drawn = base * np.exp(spread * noise) if base else spread * noise
        out[name] = __import__('jax').numpy.asarray(drawn.astype(out[name].dtype))
    for name, factor in factors.items():
        out[name] = (out[name] * factor).astype(out[name].dtype)
    return out
```

```python
from contextlib import ExitStack

import numpy as np

import concourse.bass as bass
import concourse.mybir as mybir
from concourse.alu_op_type import AluOpType as ALU

ACT = mybir.ActivationFunctionType
F32 = mybir.dt.float32
F32R = mybir.dt.float32r

P = 128
S = 1024
D = 1024
E = 2048
HEADS = 8
DV = E // HEADS
DK = DV // 2
CONV = 4
CHUNK = 128
NC = S // CHUNK
KT = D // P
ET = E // P
HALF = 512
SLOT = 1024
WINDOWS = (2, 4, 8, 16)
GROUPS = len(WINDOWS)
CG = E // GROUPS
PAD = 16
HALO = CONV - 1
EPS = 1e-5
ALPHA = 4.0 ** 0.25
FAR = 1e30

USE_GATES = 16
USE_ROWS = 18
USE_HEAD0 = 20
USES_PER_HEAD = 40
USE_LAST_OUT = USES_PER_HEAD * HEADS
USE_NORM_T = USE_LAST_OUT + 20
USE_POOL = USE_NORM_T + 16
USES_PER_GROUP = 56
SLOTS_PER_HEAD = 8
SLOT_LAST_OUT = SLOTS_PER_HEAD * HEADS - 2
SLOT_POOL = SLOTS_PER_HEAD * HEADS
SLOTS_PER_GROUP = 14

FIRST = dict(xm=(0, 2), z=4, q=8, k=10, v=12, o=16, s_xm=0, s_z=2, s_o=4, slots=6)
LATER = dict(xm=(0, 6), hn=2, out=8, z=24, q=28, k=30, v=32, o=36, s_xm=0, s_out=2, s_z=4, s_o=6, slots=8)
G_U, G_Z, G_MIX, G_OUT = 0, (8, 16), (12, 36), (20, 40)
GS_U, GS_Z, GS_MIX, GS_OUT = 0, (4, 7), (6, 11), (9, 12)

COL_W, COL_B, COL_G, COL_SKIP = 0, 4 * ET, 5 * ET, 6 * ET
COL_SCALE, COL_LNG, COL_LNB = P, P + ET, P + ET + KT
COLS = COL_LNB + KT

ACT_LN, ACT_EI, ACT_ROWS = 5, 6 + NC, 7 + 2 * NC
VEC_M, VEC_PREV, VEC_ROWS = 5, 7, 8
VEC_START, VEC_FIRST, VEC_LATER = 13, 53, 53
VEC_BETWEEN, VEC_GROUP = 41, 20
CONST_SETS, POOL_SETS = 12, 4 + GROUPS * (2 + PAD)


class Uses:

    def __init__(self, base, quarter):
        self.base, self.quarter = base, quarter

    def full(self, k):
        return self.base + (k + 1)

    def taken(self, k):
        return self.quarter + (k // 4 + 1)


START = Uses(0, 0)
LAST_OUT = Uses(USE_LAST_OUT, USE_LAST_OUT // 4)
NORM_T = Uses(USE_NORM_T, USE_NORM_T // 4)


def head_uses(h):
    if isinstance(h, int) and h == 0:
        return Uses(USE_HEAD0, USE_HEAD0 // 4)
    return Uses(h * USES_PER_HEAD, h * (USES_PER_HEAD // 4))


def group_uses(g):
    return Uses(g * USES_PER_GROUP + USE_POOL, g * (USES_PER_GROUP // 4) + USE_POOL // 4)


def build(nc, x, w_in, conv_w, conv_b, w_q, w_k, w_v, b_i, b_f, norm_g, skip, w_out,
          p_in, p_group, p_scale, p_out, ln_g, ln_b, out):
    m_rows = nc.dram_tensor("m_rows", (HEADS, S), F32, kind="Internal").ap()
    wc_rows = nc.dram_tensor("wc_rows", (HEADS, NC), F32, kind="Internal").ap()
    with ExitStack() as ctx:
        def sb(name, shape, dt=F32, where=ctx):
            return where.enter_context(nc.sbuf_tensor(name, shape, dt))

        def pb(name, shape):
            return ctx.enter_context(nc.psum_tensor(name, shape, F32))

        def sem(name):
            return ctx.enter_context(nc.semaphore(name))

        x_hi = sb("x_hi", [P, KT, S], F32R)
        x_lo = sb("x_lo", [P, KT, S], F32R)
        acc = sb("acc", [P, NC, D])
        w_raw = sb("w_raw", [P, 2, SLOT])
        w_hi = sb("w_hi", [P, 2, SLOT], F32R)
        w_lo = sb("w_lo", [P, 2, SLOT], F32R)
        gate_t = sb("gate_t", [P, 2, HALF])
        ident = sb("ident", [P, P])
        cols = sb("cols", [P, COLS])
        stats = sb("stats", [P, NC, 6])
        mv = sb("mv", [P, NC, 2])
        nhalf = sb("nhalf", [P, NC])
        rstd = sb("rstd", [P, NC])
        small = sb("small", [P, 4, NC])
        ln_stats = sb("ln_stats", [P, 2, 6])

        with ExitStack() as gates:
            e_buf = sb("e_buf", [P, 2, S], where=gates)
            f_buf = sb("f_buf", [P, 2, S], where=gates)
        y_hi = sb("y_hi", [P, 2, S], F32R)
        y_lo = sb("y_lo", [P, 2, S], F32R)

        with ExitStack() as own:
            def sa(name, shape, dt=F32):
                return sb(name, shape, dt, own)
            xm = sa("xm", [P, 2, HALO + S])
            xc = sa("xc", [P, 2, S])
            tmp_a = sa("tmp_a", [P, S])
            tmp_c = sa("tmp_c", [P, S])
            qT = sa("qT", [P, S])
            kT = sa("kT", [P, S])
            w_qkv = sa("w_qkv", [P, SLOT])
            m_bc = sa("m_bc", [P, S])
            v_sb = sa("v_sb", [P, NC, DV + 1])
            num = sa("num", [P, NC, DV + 1])
            mask = sa("mask", [P, P])
            dist = sa("dist", [P, P])
            wgt = sa("wgt", [P, P])
            sT = sa("sT", [P, P])
            kw = sa("kw", [P, P])
            state = sa("state", [P, DV + 1])
            gcol = sa("gcol", [P, NC, 4, HEADS])
            wc_bc = sa("wc_bc", [P, HEADS * NC])
            bias = sa("bias", [P, 1])

        with ExitStack() as own:
            def sB(name, shape, dt=F32):
                return sb(name, shape, dt, own)
            with ExitStack() as norm:
                g_bc = sb("g_bc", [P, D], where=norm)
                b_bc = sb("b_bc", [P, D], where=norm)
            p_hi = sB("p_hi", [P, 4, S], F32R)
            p_lo = sB("p_lo", [P, 4, S], F32R)
            u_buf = sB("u_buf", [P, 2, PAD + S])
            win_a = sB("win_a", [P, PAD + S])
            win_b = sB("win_b", [P, PAD + S])
            zz = sB("zz", [P, 2, S])
            y_t = sB("y_t", [P, 2, HALF])
            flag = sB("flag", [P, GROUPS * GROUPS])
            inv_win = sB("inv_win", [P, GROUPS])
            head_fix = sB("head_fix", [P, GROUPS * PAD])

        wide = pb("wide", [P, 4, HALF])
        ps_s = pb("ps_s", [P, HALF])
        ps_intra = pb("ps_intra", [P, HALF])
        ps_inter = pb("ps_inter", [P, HALF])
        ps_state = pb("ps_state", [P, HALF])

        par_rows = w_raw[:, 0, 0:2 * P].rearrange("p (b n) -> p b n", b=2)
        g_raw = tmp_a[:, :]
        g_hi, g_lo = y_hi[:, 0, :], y_lo[:, 0, :]
        HI, LF = slice(0, HEADS), slice(32, 32 + HEADS)
        rows = qT
        i_row, f_row = kT[HI, :], kT[LF, :]
        f_abs = tmp_c[LF, :]
        lf_row = tmp_c[HI, :]
        flat = num[:, :, :].rearrange("p c d -> p (c d)")
        bcum, m_row = flat[HI, 0:S], flat[HI, S:2 * S]
        carry, keep = xc[HI, 0, :], xc[HI, 1, :]
        m_prev, m_last = small[HI, 0, :], small[HI, 1, :]
        w_chunk = small[LF, 2, :]

        def by_chunk(row):
            return row.rearrange("p (c t) -> p c t", t=CHUNK)

        x_in = sem("x_in")
        mem_set = sem("mem_set")
        const_set = sem("const_set")
        par_in = sem("par_in")
        par_full = sem("par_full")
        gw_in = sem("gw_in")
        gw_hi = sem("gw_hi")
        gw_lo = sem("gw_lo")
        raw_in = [sem("raw_in0"), sem("raw_in1")]
        hi_ready = sem("hi_ready")
        lo_ready = sem("lo_ready")
        wide_full = sem("wide_full")
        wide_taken = [sem(f"wide_taken{b}") for b in range(4)]
        xt_hi = sem("xt_hi")
        gate_act = sem("gate_act")
        gate_vec = sem("gate_vec")
        rows_out = sem("rows_out")
        m_in = sem("m_in")
        wc_in = sem("wc_in")
        qkv_in = sem("qkv_in")
        vec_step = sem("vec_step")
        conv_ready = sem("conv_ready")
        conv_tanh = sem("conv_tanh")
        z_tanh = sem("z_tanh")
        o_used = sem("o_used")
        xc_ready = sem("xc_ready")
        y_sum = sem("y_sum")
        y_rounded = sem("y_rounded")
        y_ready = sem("y_ready")
        dist_ready = sem("dist_ready")
        wgt_ready = sem("wgt_ready")
        s_full = sem("s_full")
        s_taken = sem("s_taken")
        num_full = sem("num_full")
        intra_taken = sem("intra_taken")
        state_ready = sem("state_ready")
        var_ready = sem("var_ready")
        rstd_ready = sem("rstd_ready")
        hn_ready = sem("hn_ready")
        ln_var = sem("ln_var")
        ln_rstd = sem("ln_rstd")
        ln_x = sem("ln_x")
        x1_hi = sem("x1_hi")
        x1_lo = sem("x1_lo")
        gb_in = sem("gb_in")
        acc_scaled = sem("acc_scaled")
        pool_set = sem("pool_set")
        pool_sum = sem("pool_sum")
        pool_rounded = sem("pool_rounded")
        pool_ready = sem("pool_ready")
        ln_scaled = sem("ln_scaled")
        ln_done = sem("ln_done")
        stored = sem("stored")

        block = ctx.enter_context(nc.Block())

        def link(eng, ins, s, value):
            ins.then_inc(s, 1)
            eng.wait_ge(s, value)

        def link_taken(eng, ins, uses, k):
            link(eng, ins, wide_taken[k % 4], uses.taken(k))

        def wait_taken(eng, uses, k):
            eng.wait_ge(wide_taken[k % 4], uses.taken(k))

        def bank(k):
            return wide[:, k % 4, :]

        def half(n):
            return slice(n * HALF, (n + 1) * HALF)

        def tile(t):
            return slice(t * P, (t + 1) * P)

        def col(i):
            return cols[:, bass.ds(i, 1)]

        def slot_base(h):
            return 0 if isinstance(h, int) and h == 0 else h * SLOTS_PER_HEAD - 2

        @block.sync
        def _(sp):
            sp.wait_ge(mem_set, 1)
            sp.dma_start(par_rows[0:COL_B, 0, :], conv_w.rearrange("k (t p) -> (k t) p", p=P)).then_inc(par_in, 16)
            for c, v in ((COL_B, conv_b), (COL_G, norm_g), (COL_SKIP, skip)):
                sp.dma_start(par_rows[c:c + ET, 0, :], v.rearrange("o (t p) -> (o t) p", p=P)).then_inc(par_in, 16)
            for c, v in ((COL_SCALE, p_scale), (COL_LNG, ln_g[0:1, :]), (COL_LNB, ln_b[0:1, :])):
                sp.dma_start(par_rows[c - P:c - P + v.shape[1] // P, 1, :],
                             v.rearrange("o (t p) -> (o t) p", p=P)).then_inc(par_in, 16)
            for t in range(NC):
                sp.dma_start(acc[:, t, :], x[t * P:(t + 1) * P, :]).then_inc(x_in, 16)
            sp.wait_ge(mem_set, 2)
            gw = w_in[:, 3 * E:3 * E + 2 * HEADS].rearrange("(k p) n -> p k n", p=P)
            gv = g_raw.rearrange("p (k n) -> p k n", k=KT)
            sp.dma_start(gv[:, :, HI], gw[:, :, 0:HEADS]).then_inc(gw_in, 16)
            sp.dma_start(gv[:, :, LF], gw[:, :, HEADS:2 * HEADS]).then_inc(gw_in, 16)
            sp.dma_start(bias[HI, :], b_i.rearrange("o h -> h o")).then_inc(gw_in, 16)
            sp.dma_start(bias[LF, :], b_f.rearrange("o h -> h o")).then_inc(gw_in, 16)

            def load_slot(s, k, src):
                if k is None:
                    k = s
                else:
                    sp.wait_ge(lo_ready, s - 1)
                dst = w_raw[:, k % 2, :].rearrange("p (k n) -> p k n", k=src.shape[1])
                sp.dma_start(dst, src).then_inc(raw_in[k % 2], 16)

            def in_cols(w, c):
                return w[:, bass.ds(c, P)].rearrange("(k p) n -> p k n", p=P)

            def out_rows(w, r, n):
                return w[bass.ds(r, 2 * P), half(n)].rearrange("(k p) n -> p k n", p=P)

            def load_qkv(h):
                for i, (w, n) in enumerate(((w_q, DK), (w_k, DK), (w_v, DV))):
                    sp.dma_start(w_qkv[:, i * 2 * DK:i * 2 * DK + 2 * n].rearrange("p (k n) -> p k n", k=2),
                                 w[bass.ds(h, 1), :, :].rearrange("o (k p) n -> p (o k) n", p=P)).then_inc(qkv_in, 16)

            load_qkv(0)
            sp.wait_ge(par_full, 1)
            load_slot(0, None, in_cols(w_in, 0))
            load_slot(1, None, in_cols(w_in, P))
            for j in range(2):
                load_slot(2 + j, j, in_cols(w_in, E + j * P))
            sp.wait_ge(gate_vec, VEC_M)
            sp.dma_start(m_rows, m_row).then_inc(rows_out, 16)
            sp.wait_ge(gate_act, ACT_EI)
            sp.dma_start(wc_rows, w_chunk).then_inc(rows_out, 16)
            sp.wait_ge(rows_out, 32)
            sp.dma_start(wc_bc[:, :], wc_rows.rearrange("h c -> (h c)").partition_broadcast(P)).then_inc(wc_in, 16)
            sp.dma_start(m_bc[:, :], m_rows[0, :].partition_broadcast(P)).then_inc(m_in, 16)
            for j in range(2):
                load_slot(4 + j, j, in_cols(w_in, 2 * E + j * P))

            with sp.Fori(1, HEADS) as h:
                s0 = slot_base(h)
                for j in range(2):
                    load_slot(s0 + j, j, in_cols(w_in, h * DV + j * P))
                sp.wait_ge(wide_full, head_uses(h).full(LATER["v"] + 3 - USES_PER_HEAD))
                load_qkv(h)
                for n in range(2):
                    load_slot(s0 + 2 + n, n, out_rows(w_out, h * DV - DV, n))
                for j in range(2):
                    load_slot(s0 + 4 + j, j, in_cols(w_in, h * DV + (E + j * P)))
                sp.wait_ge(dist_ready, h * NC)
                sp.dma_start(m_bc[:, :], m_rows[bass.ds(h, 1), :].rearrange("o t -> (o t)")
                             .partition_broadcast(P)).then_inc(m_in, 16)
                for j in range(2):
                    load_slot(s0 + 6 + j, j, in_cols(w_in, h * DV + (2 * E + j * P)))

            for n in range(2):
                load_slot(SLOT_LAST_OUT + n, n, out_rows(w_out, (HEADS - 1) * DV, n))
            sp.wait_ge(state_ready, HEADS * NC)
            sp.dma_start(g_bc[:, :], ln_g[0, :].partition_broadcast(P)).then_inc(gb_in, 16)
            sp.dma_start(b_bc[:, :], ln_b[0, :].partition_broadcast(P)).then_inc(gb_in, 16)

            def group_loads(g, last):
                s0 = g * SLOTS_PER_GROUP + SLOT_POOL
                for j in range(4):
                    load_slot(s0 + j, j, in_cols(p_in, g * CG + j * P))
                for p in range(2):
                    for j in range(2):
                        load_slot(s0 + GS_Z[p] + j, GS_Z[p] + j, in_cols(p_in, g * CG + (E + (2 * p + j) * P)))
                    if p == 1:
                        for n in range(2):
                            load_slot(s0 + GS_OUT[0] + n, GS_OUT[0] + n, out_rows(p_out, g * CG, n))
                        load_mix(g, s0, 1)
                        for n in range(2):
                            load_slot(s0 + GS_OUT[1] + n, GS_OUT[1] + n, out_rows(p_out, g * CG + 2 * P, n))
                    else:
                        load_mix(g, s0, 0)

            def load_mix(g, s0, p):
                load_slot(s0 + GS_MIX[p], GS_MIX[p], p_group[bass.ds(g, 1), :, p * 2 * P:(p + 1) * 2 * P]
                          .rearrange("o (k p) n -> p (o k) n", p=P))

            with sp.Fori(0, GROUPS - 1) as g:
                group_loads(g, False)
            group_loads(GROUPS - 1, True)
            sp.wait_ge(wide_full, group_uses(GROUPS - 1).full(G_MIX[1] + 3))
            sp.dma_start(g_bc[:, :], ln_g[1, :].partition_broadcast(P)).then_inc(gb_in, 16)
            sp.dma_start(b_bc[:, :], ln_b[1, :].partition_broadcast(P)).then_inc(gb_in, 16)
            for t in range(NC):
                sp.wait_ge(ln_done, t + 1)
                sp.dma_start(out[t * P:(t + 1) * P, :], acc[:, t, :]).then_inc(stored, 16)
            sp.wait_ge(stored, 16 * NC)

        @block.gpsimd
        def _(pool):
            link(pool, pool.memset(par_rows, 0.0), mem_set, 1)
            link(pool, pool.memset(g_raw, 0.0), mem_set, 2)
            sets = [
                lambda: pool.memset(ident[:, :], 0.0),
                lambda: pool.affine_select(out=ident[:, :], in_=ident[:, :], compare_op=ALU.not_equal, fill=1.0,
                                           base=0, pattern=[[-1, P]], channel_multiplier=1),
                lambda: pool.memset(mask[:, :], 0.0),
                lambda: pool.affine_select(out=mask[:, :], in_=mask[:, :], compare_op=ALU.is_ge, fill=FAR,
                                           base=0, pattern=[[1, P]], channel_multiplier=-1),
                lambda: pool.memset(rows[:, :], 0.0),
                lambda: pool.memset(keep, 1.0),
                lambda: pool.memset(by_chunk(keep)[:, :, 0:1], 0.0),
                lambda: pool.memset(carry, 0.0),
                lambda: pool.memset(small[:, :, :], 0.0),
                lambda: pool.memset(v_sb[:, :, DV:DV + 1], 1.0),
                lambda: pool.memset(xm[:, :, 0:HALO], 0.0),
                lambda: pool.memset(nhalf[:, :], -0.5),
            ]
            assert len(sets) == CONST_SETS
            for n, f in enumerate(sets):
                link(pool, f(), const_set, n + 1)

            def make_lo(s, k):
                pool.wait_ge(hi_ready, s + 1)
                link(pool, pool.tensor_tensor(w_lo[:, k % 2, :], w_raw[:, k % 2, :],
                                              w_hi[:, k % 2, :].bitcast(F32), ALU.subtract), lo_ready, s + 1)

            def power(ready, done, n, dst, src, k):
                pool.wait_ge(ready, n)
                link(pool, pool.tensor_tensor(dst, src, nhalf[:, 0:k], ALU.pow), done, n)

            def head(h, at):
                s0 = slot_base(h)
                for k in range(2, at["slots"] + 1):
                    make_lo(s0 + k, k)
                power(var_ready, rstd_ready, h + 1, rstd[:, :], small[:, 3, :], NC)
                make_lo(s0 + at["slots"] + 1, 1)

            make_lo(0, 0)
            make_lo(1, 1)
            head(0, FIRST)
            with pool.Fori(1, HEADS) as h:
                head(h, LATER)
            for t in range(NC):
                power(ln_var, ln_rstd, t + 1, rstd[:, t:t + 1], small[:, 3, t:t + 1], 1)
            pool.wait_ge(wide_full, USE_NORM_T)
            n = 0
            for part in (u_buf[:, :, 0:PAD], win_a[:, 0:PAD], win_b[:, 0:PAD], flag[:, :]):
                n += 1
                link(pool, pool.memset(part, 0.0), pool_set, n)
            for g, win in enumerate(WINDOWS):
                n += 1
                link(pool, pool.memset(flag[:, g * GROUPS:g * GROUPS + g + 1], 1.0), pool_set, n)
                n += 1
                link(pool, pool.memset(inv_win[:, g:g + 1], 1.0 / win), pool_set, n)
                for t in range(PAD):
                    n += 1
                    link(pool, pool.memset(head_fix[:, g * PAD + t:g * PAD + t + 1], win / min(t + 1, win)), pool_set, n)
            assert n == POOL_SETS
            make_lo(SLOT_POOL, 0)
            make_lo(SLOT_POOL + 1, 1)
            with pool.Fori(0, GROUPS - 1) as g:
                s0 = g * SLOTS_PER_GROUP + SLOT_POOL
                for k in range(2, SLOTS_PER_GROUP + 2):
                    make_lo(s0 + k, k)
            s0 = (GROUPS - 1) * SLOTS_PER_GROUP + SLOT_POOL
            for k in range(2, SLOTS_PER_GROUP):
                make_lo(s0 + k, k)
            pool.wait_ge(gb_in, 64)
            for t in range(NC + 1):
                if t < NC:
                    power(ln_var, ln_rstd, NC + t + 1, rstd[:, t:t + 1], small[:, 3, t:t + 1], 1)
                if t:
                    pool.wait_ge(ln_scaled, t)
                    link(pool, pool.tensor_tensor(acc[:, t - 1, :], acc[:, t - 1, :], b_bc[:, :], ALU.add),
                         ln_done, t)

        @block.scalar
        def _(act):
            def make_hi(s, k):
                act.wait_ge(raw_in[k % 2], (s - k % 2) * 8 + 16)
                link(act, act.activation(w_hi[:, k % 2, :], w_raw[:, k % 2, :], ACT.Copy), hi_ready, s + 1)

            def take(uses, k, dst, scale=1.0):
                act.wait_ge(wide_full, uses.full(k))
                link_taken(act, act.activation(dst, bank(k), ACT.Copy, scale=scale), uses, k)

            for n in range(16):
                act.wait_ge(wide_full, n + 1)
                link(act, act.activation(x_hi[:, n % KT, half(n // KT)], bank(n), ACT.Copy), xt_hi, n + 1)
            act.wait_ge(gw_in, 64)
            link(act, act.activation(g_hi, g_raw, ACT.Copy), gw_hi, 1)
            make_hi(0, 0)
            make_hi(1, 1)
            n = 0
            for m in range(2):
                act.wait_ge(wide_full, USE_GATES + m + 1)
                n += 1
                link(act, act.activation(i_row[:, half(m)], wide[HI, m, :], ACT.Identity, bias=bias[HI, :]),
                     gate_act, n)
                link_taken(act, act.activation(f_row[:, half(m)], wide[LF, m, :], ACT.Identity, bias=bias[LF, :]),
                           START, USE_GATES + m)
            for f in (lambda: act.activation(f_abs, f_row, ACT.Abs),
                      lambda: act.activation(f_abs, f_abs, ACT.Exp, scale=-1.0),
                      lambda: act.activation(f_abs, f_abs, ACT.Ln, bias=1.0)):
                n += 1
                link(act, f(), gate_act, n)
            assert n == ACT_LN
            act.wait_ge(gate_vec, VEC_PREV)
            for c in range(NC):
                n += 1
                link(act, act.activation(rows[LF, tile(c)], m_row[:, tile(c)], ACT.Exp, scale=-1.0,
                                         bias=m_prev[:, c:c + 1]), gate_act, n)
            n += 1
            link(act, act.activation(w_chunk, by_chunk(rows[LF, :])[:, :, CHUNK - 1], ACT.Copy), gate_act, n)
            assert n == ACT_EI
            act.wait_ge(gate_vec, VEC_ROWS)
            for c in range(NC):
                n += 1
                link(act, act.activation(rows[96:96 + HEADS, tile(c)], rows[HI, tile(c)], ACT.Exp,
                                         bias=m_last[:, c:c + 1]), gate_act, n)
            n += 1
            link(act, act.activation(rows[64:64 + HEADS, :], lf_row, ACT.Exp, scale=-1.0), gate_act, n)
            assert n == ACT_ROWS
            act.preload_act_table(ACT.Tanh)

            def round_y(n, m, src):
                link(act, act.activation(y_hi[:, m % 2, half(m // 2)], src, ACT.Copy), y_rounded, n)

            def prev_y(h, ms):
                for m in ms:
                    act.wait_ge(y_sum, h * 4 + (m + 1))
                    round_y(h * 4 + (m + 1), m, tmp_c[:, half(m % 2)])

            def head(h, at, first):
                uses, s0 = head_uses(h), slot_base(h)
                for j in range(2):
                    for n in range(2):
                        k = at["xm"][j] + n
                        take(uses, k, xm[:, j, HALO + n * HALF:HALO + (n + 1) * HALF])
                        if j == 0 and n == 1:
                            make_hi(s0 + 2, 0)
                            if not first:
                                prev_y(h - 1, range(3))
                        if j == 1 and n == 0 and not first:
                            prev_y(h - 1, range(3, 4))
                make_hi(s0 + 3, 1)

                def conv_gate(j):
                    act.wait_ge(conv_ready, h * 2 + (j + 1))
                    link(act, act.activation(tmp_c[:, :], tmp_a[:, :], ACT.Tanh), conv_tanh, h * 2 + (j + 1))

                conv_gate(0)
                if not first:
                    for n in range(2):
                        act.wait_ge(wide_full, uses.full(at["out"] + NC * (n + 1) - 1))
                        make_hi(s0 + (4 + n), n)
                conv_gate(1)
                for m in range(4):
                    k = at["z"] + m
                    act.wait_ge(wide_full, uses.full(k))
                    if m >= 2:
                        wait_taken(act, uses, k - 2)
                    link(act, act.activation(gate_t[:, m % 2, :], bank(k), ACT.Tanh, scale=0.5),
                         z_tanh, h * 4 + (m + 1))
                    if m % 2:
                        make_hi(s0 + (at["s_o"] + m // 2), m // 2)
                for n in range(2):
                    take(uses, at["q"] + n, qT[:, half(n)], DK ** -0.5)
                for n in range(2):
                    take(uses, at["k"] + n, kT[:, half(n)])
                for n in range(4):
                    k = at["v"] + n
                    act.wait_ge(wide_full, uses.full(k))
                    link_taken(act, act.activation(v_sb[:, 2 * n:2 * n + 2, 0:DV],
                                                   bank(k).rearrange("p (t d) -> p t d", t=2), ACT.Copy), uses, k)

                def decay(c):
                    act.wait_ge(dist_ready, h * NC + (c + 1))
                    link(act, act.activation(wgt[:, :], dist[:, :], ACT.Exp, scale=-1.0),
                         wgt_ready, h * NC + (c + 1))

                decay(0)
                for c in range(NC):
                    if c + 1 < NC:
                        decay(c + 1)
                    act.wait_ge(num_full, h * NC + (c + 1))
                    link(act, act.activation(num[:, c, :], ps_intra[:, 0:DV + 1], ACT.Copy),
                         intra_taken, h * NC + (c + 1))
                    if c % 2:
                        m = c // 2
                        k = at["o"] + m
                        act.wait_ge(wide_full, uses.full(k))
                        if m >= 2:
                            act.wait_ge(o_used, h * 4 + (m - 1))
                        link_taken(act, act.activation(gate_t[:, m % 2, :], bank(k), ACT.Tanh, scale=0.5), uses, k)
                        if m % 2:
                            make_hi(s0 + (at["slots"] + m // 2), m // 2)

            head(0, FIRST, True)
            with act.Fori(1, HEADS) as h:
                head(h, LATER, False)
            prev_y(HEADS - 1, range(4))

            for n in range(16):
                if n >= 2:
                    act.wait_ge(x1_lo, n - 1)
                elif n == 0:
                    act.wait_ge(o_used, 4 * HEADS)
                k = n % KT
                act.wait_ge(wide_full, NORM_T.full(n))
                link_taken(act, act.activation(gate_t[:, n % 2, :], bank(n), ACT.Identity,
                                               scale=cols[:, COL_LNG + k:COL_LNG + k + 1],
                                               bias=cols[:, COL_LNB + k:COL_LNB + k + 1]), NORM_T, n)
                link(act, act.activation(x_hi[:, k, half(n // KT)], gate_t[:, n % 2, :], ACT.Copy), x1_hi, n + 1)
                if n == 3:
                    make_hi(SLOT_POOL, 0)
                    make_hi(SLOT_POOL + 1, 1)
            act.wait_ge(x1_lo, 16)
            act.wait_ge(pool_set, POOL_SETS)

            def group(g, last):
                uses, s0 = group_uses(g), g * SLOTS_PER_GROUP + SLOT_POOL

                def next_hi(k):
                    if k + 2 < SLOTS_PER_GROUP or not last:
                        make_hi(s0 + (k + 2), k)

                def round_pooled(j):
                    act.wait_ge(pool_sum, g * 4 + (j + 1))
                    link(act, act.activation(p_hi[:, j, :], win_a[:, PAD:PAD + S], ACT.Copy),
                         pool_rounded, g * 4 + (j + 1))

                def take_u(j, n):
                    take(uses, G_U + 2 * j + n, u_buf[:, j % 2, PAD + n * HALF:PAD + (n + 1) * HALF])

                def z_gate(p):
                    for m in range(4):
                        k = G_Z[p] + m
                        act.wait_ge(wide_full, uses.full(k))
                        if m >= 2:
                            wait_taken(act, uses, k - 2)
                        link(act, act.activation(gate_t[:, m % 2, :], bank(k), ACT.Tanh, scale=0.5),
                             z_tanh, g * 8 + (4 * HEADS + 4 * p + m + 1))
                        if p == 0 and m == 0:
                            round_pooled(3)
                        if m % 2:
                            next_hi(GS_Z[p] + m // 2)

                def mixed(p):
                    for m in range(4):
                        wait_taken(act, uses, G_MIX[p] + m)
                        round_y(g * 8 + (4 * HEADS + 4 * p + m + 1), m, y_t[:, m % 2, :])
                    next_hi(GS_MIX[p])

                def projected(p):
                    for n in range(2):
                        act.wait_ge(wide_full, uses.full(G_OUT[p] + NC * (n + 1) - 1))
                        next_hi(GS_OUT[p] + n)

                take_u(0, 0)
                for j in range(4):
                    if j:
                        take_u(j, 0)
                        round_pooled(j - 1)
                    take_u(j, 1)
                    next_hi(GS_U + j)
                z_gate(0)
                mixed(0)
                z_gate(1)
                projected(0)
                mixed(1)
                if not last:
                    projected(1)

            with act.Fori(0, GROUPS - 1) as g:
                group(g, False)
            group(GROUPS - 1, True)

        @block.vector
        def _(dve):
            base, steps = [0], [0]

            def step(ins, wait=True):
                steps[0] += 1
                ins.then_inc(vec_step, 1)
                if wait:
                    dve.wait_ge(vec_step, base[0] + steps[0])

            def part(start, count, f):
                base[0], steps[0] = start, 0
                f()
                assert steps[0] == count, (steps[0], count)

            def residual(uses, k, t, n):
                dve.wait_ge(wide_full, uses.full(k))
                link_taken(dve, dve.tensor_tensor(acc[:, t, half(n)], bank(k), acc[:, t, half(n)], ALU.add), uses, k)

            def start():
                dve.wait_ge(par_full, 1)
                step(dve.tensor_copy(cols[:, :], ps_s[:, 0:COLS]))
                for a, b, f in ((COL_W, COL_G, 0.5), (COL_G, COL_SKIP, 0.25), (COL_SKIP, COL_SCALE, 0.5),
                                (COL_SCALE, COL_LNG, 0.5)):
                    step(dve.tensor_scalar(cols[:, a:b], cols[:, a:b], f, None, ALU.mult))
                for n in range(16):
                    dve.wait_ge(xt_hi, n + 1)
                    link_taken(dve, dve.tensor_tensor(x_lo[:, n % KT, half(n // KT)], bank(n),
                                                      x_hi[:, n % KT, half(n // KT)].bitcast(F32), ALU.subtract),
                               START, n)
                dve.wait_ge(gw_hi, 1)
                link(dve, dve.tensor_tensor(g_lo, g_raw, g_hi.bitcast(F32), ALU.subtract), gw_lo, 1)
                for t in range(NC):
                    step(dve.tensor_scalar(acc[:, t, :], acc[:, t, :], ALPHA, None, ALU.mult))
                dve.wait_ge(const_set, CONST_SETS)
                dve.wait_ge(gate_act, ACT_LN)
                n = 0

                def gate(ins):
                    nonlocal n
                    n += 1
                    link(dve, ins, gate_vec, n)

                gate(dve.scalar_tensor_tensor(out=lf_row, in0=f_row, scalar=0.0, in1=f_abs,
                                              op0=ALU.min, op1=ALU.subtract))
                gate(dve.tensor_tensor_scan(bcum, keep, lf_row, 0.0, ALU.mult, ALU.add))
                gate(dve.tensor_tensor(rows[HI, :], i_row, bcum, ALU.subtract))
                gate(dve.tensor_copy(by_chunk(carry)[:, 1:NC, 0], by_chunk(bcum)[:, 0:NC - 1, CHUNK - 1]))
                gate(dve.tensor_tensor_scan(m_row, carry, rows[HI, :], 0.0, ALU.add, ALU.max))
                assert n == VEC_M
                gate(dve.tensor_tensor(m_prev[:, 1:NC], by_chunk(m_row)[:, 0:NC - 1, CHUNK - 1],
                                       by_chunk(bcum)[:, 0:NC - 1, CHUNK - 1], ALU.add))
                gate(dve.tensor_scalar(m_last, by_chunk(m_row)[:, :, CHUNK - 1], -1.0, None, ALU.mult))
                assert n == VEC_PREV
                gate(dve.tensor_tensor(lf_row, bcum, m_row, ALU.add))
                assert n == VEC_ROWS
                for m in range(2):
                    dve.wait_ge(wide_full, USE_ROWS + m + 1)
                    link_taken(dve, dve.tensor_copy(
                        gcol[:, 4 * m:4 * m + 4, :, :],
                        bank(USE_ROWS + m).rearrange("p (c q r) -> p c q r", c=4, q=4)[:, :, :, 0:HEADS]),
                        START, USE_ROWS + m)
                dve.wait_ge(wc_in, 16)

            part(0, VEC_START, start)

            def gated_output(h, uses, first_use):
                def summed(m):
                    k, j, n = first_use + m, m % 2, m // 2
                    dve.wait_ge(wide_full, uses.full(k))
                    link_taken(dve, dve.scalar_tensor_tensor(
                        out=tmp_c[:, half(m % 2)], in0=bank(k), scalar=col(h * 2 + (COL_G + j)),
                        in1=e_buf[:, j, half(n)], op0=ALU.mult, op1=ALU.mult), uses, k)
                    link(dve, dve.tensor_tensor(tmp_c[:, half(m % 2)], tmp_c[:, half(m % 2)],
                                                f_buf[:, j, half(n)], ALU.add), y_sum, h * 4 + (m + 1))

                for m in range(5):
                    if m < 4:
                        summed(m)
                    if m:
                        lo_part(h * 4 + m, m - 1, tmp_c[:, half((m - 1) % 2)])

            def lo_part(n, m, src):
                dve.wait_ge(y_rounded, n)
                dst = (slice(None), m % 2, half(m // 2))
                link(dve, dve.tensor_tensor(y_lo[dst], src, y_hi[dst].bitcast(F32), ALU.subtract), y_ready, n)

            def head(h, at, first):
                uses = head_uses(h)

                def conv(j):
                    def tap(i):
                        if i == 0:
                            for n in range(2):
                                wait_taken(dve, uses, at["xm"][j] + n)
                            step(dve.tensor_scalar(tmp_a[:, :], xm[:, j, HALO:HALO + S],
                                                   col(h * 2 + (COL_W + 3 * ET + j)), col(h * 2 + (COL_B + j)),
                                                   ALU.mult, ALU.add))
                            return
                        w = HALO - i
                        ins = dve.scalar_tensor_tensor(
                            out=tmp_a[:, :], in0=xm[:, j, w:w + S], scalar=col(h * 2 + (COL_W + w * ET + j)),
                            in1=tmp_a[:, :], op0=ALU.mult, op1=ALU.add)
                        if i < HALO:
                            step(ins)
                        else:
                            link(dve, ins, conv_ready, h * 2 + (j + 1))

                    def gate():
                        dve.wait_ge(conv_tanh, h * 2 + (j + 1))
                        link(dve, dve.scalar_tensor_tensor(out=xc[:, j, :], in0=tmp_c[:, :], scalar=1.0,
                                                           in1=tmp_a[:, :], op0=ALU.add, op1=ALU.mult),
                             xc_ready, h * 2 + (j + 1))
                    return [lambda i=i: tap(i) for i in range(CONV)] + [gate]

                work = conv(0) + conv(1)
                if first:
                    for f in work:
                        f()
                else:
                    gated_output(h - 1, uses, at["hn"])
                    for n in range(2):
                        for t in range(NC):
                            residual(uses, at["out"] + n * NC + t, t, n)
                            if t % 2 and len(work) > 2:
                                work.pop(0)()
                    for f in work:
                        f()
                for m in range(4):
                    k, j, n = at["z"] + m, m // 2, m % 2
                    dve.wait_ge(z_tanh, h * 4 + (m + 1))
                    link_taken(dve, dve.scalar_tensor_tensor(
                        out=e_buf[:, j, half(n)], in0=gate_t[:, m % 2, :], scalar=1.0, in1=bank(k),
                        op0=ALU.add, op1=ALU.mult), uses, k)
                    if n:
                        step(dve.scalar_tensor_tensor(out=f_buf[:, j, :], in0=xc[:, j, :],
                                                      scalar=col(h * 2 + (COL_SKIP + j)), in1=e_buf[:, j, :],
                                                      op0=ALU.mult, op1=ALU.mult))
                step(dve.memset(state[:, :], 0.0))

                def gate_col(c, q):
                    return gcol[:, c, q, bass.ds(h, 1)]

                def distance(c):
                    link(dve, dve.scalar_tensor_tensor(out=dist[:, :], in0=m_bc[:, tile(c)], scalar=gate_col(c, 0),
                                                       in1=mask[:, :], op0=ALU.subtract, op1=ALU.add),
                         dist_ready, h * NC + (c + 1))

                dve.wait_ge(m_in, h * 16 + 16)
                distance(0)
                for c in range(NC):
                    dve.wait_ge(s_full, h * NC + (c + 1))
                    dve.wait_ge(wgt_ready, h * NC + (c + 1))
                    step(dve.tensor_tensor(sT[:, :], ps_s[:, 0:P], wgt[:, :], ALU.mult))
                    link(dve, dve.tensor_scalar(kw[:, :], ps_s[:, P:2 * P], gate_col(c, 3), None, ALU.mult),
                         s_taken, h * NC + (c + 1))
                    if c + 1 < NC:
                        distance(c + 1)
                    dve.wait_ge(num_full, h * NC + (c + 1))
                    dve.wait_ge(intra_taken, h * NC + (c + 1))
                    step(dve.scalar_tensor_tensor(out=num[:, c, :], in0=ps_inter[:, 0:DV + 1], scalar=gate_col(c, 1),
                                                  in1=num[:, c, :], op0=ALU.mult, op1=ALU.add))
                    link(dve, dve.scalar_tensor_tensor(out=state[:, :], in0=state[:, :],
                                                       scalar=wc_bc[:, bass.ds(h * NC + c, 1)],
                                                       in1=ps_state[:, 0:DV + 1], op0=ALU.mult, op1=ALU.add),
                         state_ready, h * NC + (c + 1))
                    step(dve.bn_stats(stats[:, c, :], num[:, c, 0:DV]))
                    if c % 2:
                        m = c // 2
                        wait_taken(dve, uses, at["o"] + m)
                        j, n = m // 2, m % 2
                        link(dve, dve.scalar_tensor_tensor(out=e_buf[:, j, half(n)], in0=gate_t[:, m % 2, :],
                                                           scalar=1.0, in1=e_buf[:, j, half(n)],
                                                           op0=ALU.add, op1=ALU.mult), o_used, h * 4 + (m + 1))
                big, r, r2, var = (small[:, i, :] for i in range(4))
                step(dve.scalar_tensor_tensor(out=big, in0=num[:, :, DV], scalar=-1.0,
                                              in1=gcol[:, :, 2, bass.ds(h, 1)].rearrange("p c o -> p (c o)"),
                                              op0=ALU.mult, op1=ALU.max), wait=False)
                for c in range(NC):
                    step(dve.bn_aggr(mv[:, c, :], stats[:, c, :]), wait=c == NC - 1)
                step(dve.tensor_tensor(big, num[:, :, DV], big, ALU.max))
                step(dve.reciprocal(r, big))
                step(dve.tensor_tensor(r2, r, r, ALU.mult))
                step(dve.tensor_tensor(var, r2, mv[:, :, 1], ALU.mult))
                link(dve, dve.tensor_scalar(var, var, EPS, None, ALU.add), var_ready, h + 1)
                dve.wait_ge(rstd_ready, h + 1)
                step(dve.tensor_tensor(r2, r, rstd[:, :], ALU.mult))
                for c in range(NC):
                    ins = dve.tensor_scalar(num[:, c, 0:DV], num[:, c, 0:DV], mv[:, c, 0:1], r2[:, c:c + 1],
                                            ALU.subtract, ALU.mult)
                    if c % 4 == 3:
                        link(dve, ins, hn_ready, h * 2 + (c // 4 + 1))
                    else:
                        step(ins)

            part(VEC_START, VEC_FIRST, lambda: head(0, FIRST, True))
            with dve.Fori(1, HEADS) as h:
                part(h * VEC_LATER + (VEC_START + VEC_FIRST - VEC_LATER), VEC_LATER, lambda: head(h, LATER, False))

            def norm_stats(t, n):
                for i in range(2):
                    step(dve.bn_stats(ln_stats[:, i, :], acc[:, t, half(i)]))
                step(dve.bn_aggr(mv[:, t, :], ln_stats[:, :, :].rearrange("p a b -> p (a b)")))
                link(dve, dve.tensor_scalar(small[:, 3, t:t + 1], mv[:, t, 1:2], EPS, None, ALU.add), ln_var, n + t + 1)

            def normed(t, n):
                dve.wait_ge(ln_rstd, n + t + 1)
                link(dve, dve.tensor_scalar(acc[:, t, :], acc[:, t, :], mv[:, t, 0:1], rstd[:, t:t + 1],
                                            ALU.subtract, ALU.mult), ln_x, n + t + 1)

            def between():
                gated_output(HEADS - 1, LAST_OUT, 0)
                for t in range(NC + 1):
                    if t < NC:
                        for n in range(2):
                            residual(LAST_OUT, 4 + 2 * t + n, t, n)
                        norm_stats(t, 0)
                    if t:
                        normed(t - 1, 0)
                for n in range(16):
                    dve.wait_ge(x1_hi, n + 1)
                    dst = (slice(None), n % KT, half(n // KT))
                    link(dve, dve.tensor_tensor(x_lo[dst], gate_t[:, n % 2, :], x_hi[dst].bitcast(F32),
                                                ALU.subtract), x1_lo, n + 1)
                dve.wait_ge(gb_in, 32)
                for v in (g_bc, b_bc):
                    step(dve.tensor_scalar(v[:, :], v[:, :], ALPHA, None, ALU.mult))
                for t in range(NC):
                    step(dve.tensor_tensor(acc[:, t, :], acc[:, t, :], g_bc[:, :], ALU.mult))
                    ins = dve.tensor_tensor(acc[:, t, :], acc[:, t, :], b_bc[:, :], ALU.add)
                    if t + 1 < NC:
                        step(ins)
                    else:
                        link(dve, ins, acc_scaled, 1)
                dve.wait_ge(pool_set, POOL_SETS)

            at_pool = VEC_START + VEC_FIRST + (HEADS - 1) * VEC_LATER
            part(at_pool, VEC_BETWEEN, between)

            def group(g, last):
                uses = group_uses(g)
                for j in range(4):
                    for n in range(2):
                        wait_taken(dve, uses, G_U + 2 * j + n)
                    src = u_buf[:, j % 2, :]
                    for level, dst in enumerate((win_a, win_b, win_a, win_b)):
                        back = PAD - (1 << level)
                        step(dve.scalar_tensor_tensor(out=dst[:, PAD:PAD + S], in0=src[:, back:back + S],
                                                      scalar=flag[:, bass.ds(g * GROUPS + level, 1)],
                                                      in1=src[:, PAD:PAD + S], op0=ALU.mult, op1=ALU.add))
                        src = dst
                    step(dve.tensor_tensor(win_b[:, PAD:2 * PAD], win_b[:, PAD:2 * PAD],
                                           head_fix[:, bass.ds(g * PAD, PAD)], ALU.mult))
                    link(dve, dve.scalar_tensor_tensor(out=win_a[:, PAD:PAD + S], in0=win_b[:, PAD:PAD + S],
                                                       scalar=inv_win[:, bass.ds(g, 1)],
                                                       in1=u_buf[:, j % 2, PAD:PAD + S],
                                                       op0=ALU.mult, op1=ALU.subtract), pool_sum, g * 4 + (j + 1))
                    dve.wait_ge(pool_rounded, g * 4 + (j + 1))
                    link(dve, dve.tensor_tensor(p_lo[:, j, :], win_a[:, PAD:PAD + S], p_hi[:, j, :].bitcast(F32),
                                                ALU.subtract), pool_ready, g * 4 + (j + 1))

                def z_gate(p):
                    for m in range(4):
                        k = G_Z[p] + m
                        dve.wait_ge(z_tanh, g * 8 + (4 * HEADS + 4 * p + m + 1))
                        link_taken(dve, dve.scalar_tensor_tensor(
                            out=zz[:, m // 2, half(m % 2)], in0=gate_t[:, m % 2, :], scalar=1.0, in1=bank(k),
                            op0=ALU.add, op1=ALU.mult), uses, k)

                def mixed(p):
                    for m in range(5):
                        if m < 4:
                            k = G_MIX[p] + m
                            dve.wait_ge(wide_full, uses.full(k))
                            link_taken(dve, dve.scalar_tensor_tensor(
                                out=y_t[:, m % 2, :], in0=bank(k), scalar=col(g * 4 + (COL_SCALE + 2 * p + m % 2)),
                                in1=zz[:, m % 2, half(m // 2)], op0=ALU.mult, op1=ALU.mult), uses, k)
                        if m:
                            lo_part(g * 8 + (4 * HEADS + 4 * p + m), m - 1, y_t[:, (m - 1) % 2, :])

                def project(p):
                    for n in range(2):
                        for t in range(NC):
                            residual(uses, G_OUT[p] + n * NC + t, t, n)

                z_gate(0)
                mixed(0)
                z_gate(1)
                project(0)
                mixed(1)
                if not last:
                    project(1)
                    return
                for t in range(NC + 1):
                    if t < NC:
                        for n in range(2):
                            residual(uses, G_OUT[1] + 2 * t + n, t, n)
                        norm_stats(t, NC)
                    if t:
                        normed(t - 1, NC)
                        if t == 1:
                            dve.wait_ge(gb_in, 64)
                        link(dve, dve.tensor_tensor(acc[:, t - 1, :], acc[:, t - 1, :], g_bc[:, :], ALU.mult),
                             ln_scaled, t)

            at_pool += VEC_BETWEEN
            with dve.Fori(0, GROUPS - 1) as g:
                part(g * VEC_GROUP + at_pool, VEC_GROUP, lambda: group(g, False))
            part(at_pool + (GROUPS - 1) * VEC_GROUP, VEC_GROUP + 3 * NC, lambda: group(GROUPS - 1, True))

        @block.tensor
        def _(pe):
            def free(uses, k):
                if uses is not START or k >= 4:
                    pe.wait_ge(wide_taken[k % 4], uses.taken(k - 4))

            def split(dst, a, b, first, last):
                pe.matmul(dst, a[0], b[0], start=first, stop=False)
                pe.matmul(dst, a[0], b[1], start=False, stop=False)
                return pe.matmul(dst, a[1], b[0], start=False, stop=last)

            def in_product(uses, k, n, w, between=None):
                free(uses, k)
                for t in range(KT):
                    mm = split(bank(k), [v[:, tile(t)] for v in w], [v[:, t, half(n)] for v in (x_hi, x_lo)],
                               t == 0, t == KT - 1)
                    if t == KT - 1:
                        mm.then_inc(wide_full, 1)
                    if between and t % 4 == 3:
                        between()

            def slot(s0, k):
                pe.wait_ge(lo_ready, s0 + (k + 1))
                return w_hi[:, k % 2, :], w_lo[:, k % 2, :]

            def in_slot(uses, s0, ks, k, between=None):
                w = slot(s0, ks)
                for n in range(2):
                    in_product(uses, k + n, n, w, between)

            def out_product(uses, k, w, t):
                free(uses, k)
                for j in range(2):
                    mm = split(bank(k), [v[:, j, tile(t)] for v in (y_hi, y_lo)],
                               [v[:, half(j)] for v in w], j == 0, j == 1)
                mm.then_inc(wide_full, 1)

            def wait_y(n, t):
                if t % 4 == 0:
                    pe.wait_ge(y_ready, n + 2 + t // 2)

            def project(uses, k, s0, ks, y_before):
                for n in range(2):
                    w = slot(s0, ks + n)
                    for t in range(NC):
                        if n == 0:
                            wait_y(y_before, t)
                        out_product(uses, k + n * NC + t, w, t)

            def project_by_token(uses, k, s0, ks, y_before):
                ws = [slot(s0, ks + n) for n in range(2)]
                for t in range(NC):
                    wait_y(y_before, t)
                    for n in range(2):
                        out_product(uses, k + 2 * t + n, ws[n], t)

            def turn(uses, k, srcs):
                free(uses, k)
                for i, src in enumerate(srcs):
                    mm = pe.transpose(bank(k)[:, tile(i)], src, ident[:, :])
                mm.then_inc(wide_full, 1)

            pe.wait_ge(const_set, 2)
            pe.wait_ge(par_in, 16 * 7)
            pe.transpose(ps_s[:, 0:P], par_rows[:, 0, :], ident[:, :])
            pe.transpose(ps_s[:, P:2 * P], par_rows[:, 1, :], ident[:, :]).then_inc(par_full, 1)
            for m in range(2):
                for t in range(KT):
                    if t == 0:
                        pe.wait_ge(x_in, 16 * NC)
                    turn(START, m * KT + t, [acc[:, 4 * m + i, tile(t)] for i in range(4)])
            pe.wait_ge(gw_lo, 1)
            for n in range(2):
                in_product(START, USE_GATES + n, n, (g_hi, g_lo))

            def prev_out(h, uses, at):
                for m in range(4):
                    if m % 2 == 0:
                        pe.wait_ge(hn_ready, h * 2 + (m // 2 + 1))
                    turn(uses, at + m, [num[:, 4 * (m // 2) + i, (m % 2) * P:(m % 2 + 1) * P] for i in range(4)])

            def head(h, at, first):
                uses, s0 = head_uses(h), slot_base(h)
                in_slot(uses, s0, 0, at["xm"][0])
                if not first:
                    prev_out(h - 1, uses, at["hn"])
                in_slot(uses, s0, 1, at["xm"][1])
                if not first:
                    project(uses, at["out"], s0, at["s_out"], h * 4 - 4)
                for j in range(2):
                    in_slot(uses, s0, at["s_z"] + j, at["z"] + 2 * j)
                pe.wait_ge(qkv_in, h * 48 + 48)
                pe.wait_ge(xc_ready, h * 2 + 2)
                for i, part in enumerate(("q", "k")):
                    for n in range(2):
                        k = at[part] + n
                        free(uses, k)
                        for j in range(2):
                            w = (2 * i + j) * DK
                            mm = pe.matmul(bank(k), w_qkv[:, w:w + DK], xc[:, j, half(n)], start=j == 0, stop=j == 1)
                        mm.then_inc(wide_full, 1)
                for n in range(4):
                    k = at["v"] + n
                    free(uses, k)
                    for i in range(2):
                        for j in range(2):
                            w = 4 * DK + j * DV
                            at_t = HALO + (2 * n + i) * P
                            mm = pe.matmul(bank(k)[:, i * DV:(i + 1) * DV], xm[:, j, at_t:at_t + P],
                                           w_qkv[:, w:w + DV], start=j == 0, stop=j == 1)
                    mm.then_inc(wide_full, 1)

                def scores(c):
                    pe.transpose(ps_s[:, P:2 * P], kT[:, tile(c)], ident[:, :])
                    pe.matmul(ps_s[:, 0:P], kT[:, tile(c)], qT[:, tile(c)], start=True, stop=True).then_inc(s_full, 1)

                def outputs(c):
                    pe.wait_ge(s_taken, h * NC + (c + 1))
                    if not (first and c == 0):
                        pe.wait_ge(state_ready, h * NC + c)
                    pe.matmul(ps_intra[:, 0:DV + 1], sT[:, :], v_sb[:, c, :], start=True, stop=True)
                    pe.matmul(ps_inter[:, 0:DV + 1], qT[:, tile(c)], state[:, :], start=True, stop=True)
                    pe.matmul(ps_state[:, 0:DV + 1], kw[:, :], v_sb[:, c, :], start=True, stop=True).then_inc(num_full, 1)

                for n in range(2):
                    wait_taken(pe, uses, at["k"] + n)
                for n in range(4):
                    wait_taken(pe, uses, at["v"] + n)
                scores(0)
                chunk = [0]

                def core():
                    c = chunk[0]
                    outputs(c)
                    if c + 1 < NC:
                        scores(c + 1)
                    chunk[0] += 1

                for j in range(2):
                    in_slot(uses, s0, at["s_o"] + j, at["o"] + 2 * j, core)

            for m in range(2):
                if m == 0:
                    pe.wait_ge(gate_act, ACT_ROWS)
                turn(START, USE_ROWS + m, [rows[:, tile(4 * m + i)] for i in range(4)])
            head(0, FIRST, True)
            with pe.Fori(1, HEADS) as h:
                head(h, LATER, False)
            prev_out(HEADS - 1, LAST_OUT, 0)
            project_by_token(LAST_OUT, 4, SLOT_LAST_OUT, 0, 4 * HEADS - 4)
            for n in range(16):
                if n % KT == 0:
                    pe.wait_ge(ln_x, 4 * (n // KT) + 4)
                turn(NORM_T, n, [acc[:, 4 * (n // KT) + i, tile(n % KT)] for i in range(4)])
            pe.wait_ge(x1_lo, 16)

            def group(g, last):
                uses, s0 = group_uses(g), g * SLOTS_PER_GROUP + SLOT_POOL
                y0 = g * 8 + 4 * HEADS
                for j in range(4):
                    in_slot(uses, s0, GS_U + j, G_U + 2 * j)

                def z_and_mix(p):
                    for j in range(2):
                        in_slot(uses, s0, GS_Z[p] + j, G_Z[p] + 2 * j)
                    if p:
                        project(uses, G_OUT[0], s0, GS_OUT[0], y0)
                    else:
                        pe.wait_ge(pool_ready, g * 4 + 4)
                    w = slot(s0, GS_MIX[p])
                    for m in range(4):
                        n, j, k = m // 2, m % 2, G_MIX[p] + m
                        free(uses, k)
                        for t in range(4):
                            at = t * 2 * P + j * P
                            mm = split(bank(k), [v[:, at:at + P] for v in w],
                                       [v[:, t, half(n)] for v in (p_hi, p_lo)], t == 0, t == 3)
                        mm.then_inc(wide_full, 1)

                z_and_mix(0)
                z_and_mix(1)
                (project_by_token if last else project)(uses, G_OUT[1], s0, GS_OUT[1], y0 + 4)

            with pe.Fori(0, GROUPS - 1) as g:
                group(g, False)
            group(GROUPS - 1, True)


_INS = ("x", "mlstm_w_in", "mlstm_conv_w", "mlstm_conv_b", "mlstm_w_q", "mlstm_w_k", "mlstm_w_v", "mlstm_b_i",
        "mlstm_b_f", "mlstm_norm_g", "mlstm_skip", "mlstm_w_out", "pool_w_in", "pool_w_group", "pool_scale",
        "pool_w_out", "post_ln_g", "post_ln_b")
_KEEP_LAYER_AXIS = ("mlstm_conv_b", "mlstm_b_i", "mlstm_b_f", "mlstm_norm_g", "mlstm_skip", "pool_scale",
                    "post_ln_g", "post_ln_b")


def kernel(**inputs):
    from concourse import bacc
    from concourse.bass_utils import run_bass_kernel_spmd

    nc = bacc.Bacc("TRN2", target_bir_lowering=False, num_devices=1)
    arrays, args = {}, []
    for name in _INS:
        a = np.ascontiguousarray(inputs[name])
        if name not in _KEEP_LAYER_AXIS:
            a = a[0]
        arrays[f"in_{name}"] = a
        args.append(nc.dram_tensor(f"in_{name}", a.shape, F32, kind="ExternalInput").ap())
    out = nc.dram_tensor("out", (S, D), F32, kind="ExternalOutput").ap()
    build(nc, *args, out)
    got = run_bass_kernel_spmd(nc, [arrays], core_ids=[0])
    return got.results[0]["out"].reshape(1, S, D)
```

```python
from contextlib import ExitStack

import numpy as np

import concourse.bass as bass
import concourse.mybir as mybir
from concourse.alu_op_type import AluOpType as ALU

ACT = mybir.ActivationFunctionType
F32 = mybir.dt.float32
F32R = mybir.dt.float32r

P = 128
S = 1024
D = 1024
E = 2048
HEADS = 8
DV = E // HEADS
DK = DV // 2
CONV = 4
CHUNK = 128
NC = S // CHUNK
KT = D // P
ET = E // P
HALF = 512
SLOT = 1024
WINDOWS = (2, 4, 8, 16)
GROUPS = len(WINDOWS)
CG = E // GROUPS
PAD = 16
HALO = CONV - 1
EPS = 1e-5
ALPHA = 4.0 ** 0.25
FAR = 1e30

USE_X = [*range(8), *range(11, 19)]
USE_PAR = (8, 9)
USE_GATES = (10, 19)
USE_HEAD0 = 20
USES_PER_HEAD = 40
USE_LAST_OUT = USES_PER_HEAD * HEADS
BRIDGE = [("T", 0), ("T", 1), *(("O", i) for i in range(4)), ("T", 2), ("T", 3), *(("O", i) for i in range(4, 12)),
          *(("X", i) for i in range(3)),
          ("O", 12), ("O", 13), *(("X", i) for i in range(3, 6)), ("O", 14), ("O", 15), ("X", 6), ("X", 7),
          ("U", 0), *(("X", i) for i in range(8, 11)), ("U", 1), *(("X", i) for i in range(11, 16))]
BRIDGE_T, BRIDGE_O, BRIDGE_X, BRIDGE_U = ([k for k, (kind, _) in enumerate(BRIDGE) if kind == which]
                                          for which in "TOXU")
USE_POOL = USE_LAST_OUT + len(BRIDGE) - 2
LAST_PROJECT = [(0, 0), (1, 0), (0, 1), (1, 1), *((t, n) for t in range(2, NC) for n in range(2))]
USES_PER_GROUP = 56
SLOTS_PER_HEAD = 8
SLOT_LAST_OUT = SLOTS_PER_HEAD * HEADS - 2
SLOT_POOL = SLOTS_PER_HEAD * HEADS
SLOTS_PER_GROUP = 14

FIRST = dict(xm=(0, 2), z=4, q=8, k=12, v=(10, 11, 14, 15), o=16, s_xm=0, s_z=2, s_o=4, slots=6)
LATER = dict(xm=(0, 6), hn=2, out=8, z=24, q=28, k=32, v=(30, 31, 34, 35), o=36, s_xm=0, s_out=2, s_z=4, s_o=6, slots=8)
G_U, G_Z, G_MIX, G_OUT = 0, (8, 16), (12, 36), (20, 40)
GS_U, GS_Z, GS_MIX, GS_OUT = 0, (4, 7), (6, 11), (9, 12)

COL_W, COL_B, COL_G, COL_SKIP = 0, 4 * ET, 5 * ET, 6 * ET
COL_SCALE, COL_LNG, COL_LNB = P, P + ET, P + ET + KT
COLS = COL_LNB + KT

ACT_LN, ACT_EI, ACT_ROWS = 5, 7 + NC, 7 + 2 * NC
VEC_M, VEC_PREV, VEC_ROWS = 5, 7, 8
VEC_START, VEC_FIRST, VEC_LATER = 4, 71, 61
VEC_BETWEEN, VEC_GROUP = 2, 20
SET_IDENT, SET_PAR, SET_GATES, CONST_SETS = 2, 3, 4, 14
POOL_SETS = 4 + 3 * GROUPS + sum(win - 1 for win in WINDOWS)


LATE = NC - 1


class Uses:

    def __init__(self, base, quarter):
        self.base, self.quarter = base, quarter

    def full(self, k):
        return self.base + (k + 1)

    def taken(self, k):
        return self.quarter + (k // 4 + 1)


START = Uses(0, 0)
BETWEEN = Uses(USE_LAST_OUT, USE_LAST_OUT // 4)


def head_uses(h):
    if isinstance(h, int) and h == 0:
        return Uses(USE_HEAD0, USE_HEAD0 // 4)
    return Uses(h * USES_PER_HEAD, h * (USES_PER_HEAD // 4))


def group_uses(g):
    return Uses(g * USES_PER_GROUP + USE_POOL, g * (USES_PER_GROUP // 4) + USE_POOL // 4)


def build(nc, x, w_in, conv_w, conv_b, w_q, w_k, w_v, b_i, b_f, norm_g, skip, w_out,
          p_in, p_group, p_scale, p_out, ln_g, ln_b, out):
    m_rows = nc.dram_tensor("m_rows", (HEADS, S), F32, kind="Internal").ap()
    wc_rows = nc.dram_tensor("wc_rows", (HEADS, NC), F32, kind="Internal").ap()
    with ExitStack() as ctx:
        def sb(name, shape, dt=F32, where=ctx):
            return where.enter_context(nc.sbuf_tensor(name, shape, dt))

        def pb(name, shape):
            return ctx.enter_context(nc.psum_tensor(name, shape, F32))

        def sem(name):
            return ctx.enter_context(nc.semaphore(name))

        with ExitStack() as behind:
            normed_out = sb("normed_out", [P, NC, D], where=behind)
        x_hi = sb("x_hi", [P, KT, S], F32R)
        x_lo = sb("x_lo", [P, KT, S], F32R)
        acc = sb("acc", [P, NC, D])
        w_raw = sb("w_raw", [P, 2, SLOT])
        w_hi = sb("w_hi", [P, 2, SLOT], F32R)
        w_lo = sb("w_lo", [P, 2, SLOT], F32R)
        gate_t = sb("gate_t", [P, 2, HALF])
        ident = sb("ident", [P, P])
        cols = sb("cols", [P, COLS])
        stats = sb("stats", [P, NC, 6])
        mv = sb("mv", [P, NC, 2])
        nhalf = sb("nhalf", [P, NC])
        rstd = sb("rstd", [P, NC])
        small = sb("small", [P, 4, NC])
        ln_stats = sb("ln_stats", [P, 2, 6])

        with ExitStack() as gates:
            e_buf = sb("e_buf", [P, 2, S], where=gates)
            f_buf = sb("f_buf", [P, 2, S], where=gates)
        y_hi = sb("y_hi", [P, 2, S], F32R)
        y_lo = sb("y_lo", [P, 2, S], F32R)

        with ExitStack() as own:
            def sa(name, shape, dt=F32):
                return sb(name, shape, dt, own)
            xm = sa("xm", [P, 2, HALO + S])
            with ExitStack() as whole:
                xc = sb("xc", [P, 2, S], where=whole)
            xc_lo = sa("xc_lo", [P, 2, S], F32R)
            with ExitStack() as conv:
                tmp_a = sb("tmp_a", [P, S], where=conv)
                tmp_c = sb("tmp_c", [P, S], where=conv)
            xm_hi = sa("xm_hi", [P, 2, HALF], F32R)
            xm_lo = sa("xm_lo", [P, 2, HALF], F32R)
            with ExitStack() as whole:
                w_qkv = sb("w_qkv", [P, SLOT], where=whole)
            qkv_lo = sa("qkv_lo", [P, SLOT], F32R)
            qkv_hi = sa("qkv_hi", [P, SLOT], F32R)
            qT = sa("qT", [P, S])
            kT = sa("kT", [P, S])
            m_bc = sa("m_bc", [P, S])
            v_sb = sa("v_sb", [P, NC, DV + 1])
            with ExitStack() as early:
                xc_hi = sb("xc_hi", [P, 2, S], F32R, early)
            num = sa("num", [P, NC, DV + 1])
            mask = sa("mask", [P, P])
            dist = sa("dist", [P, P])
            wgt = sa("wgt", [P, P])
            sT = sa("sT", [P, P])
            kw = sa("kw", [P, P])
            state = sa("state", [P, DV + 1])
            gcol = sa("gcol", [P, NC, 4, HEADS])
            wc_bc = sa("wc_bc", [P, HEADS * NC])
            bias = sa("bias", [P, 1])

        with ExitStack() as own:
            def sB(name, shape, dt=F32):
                return sb(name, shape, dt, own)
            with ExitStack() as ahead:
                x_new = sb("x_new", [P, 4, HALF], where=ahead)
            with ExitStack() as behind:
                g_bc = sb("g_bc", [P, D], where=behind)
                b_bc = sb("b_bc", [P, D], where=behind)
            p_hi = sB("p_hi", [P, 4, S], F32R)
            p_lo = sB("p_lo", [P, 4, S], F32R)
            u_buf = sB("u_buf", [P, 2, PAD + S])
            win_a = sB("win_a", [P, PAD + S])
            win_b = sB("win_b", [P, PAD + S])
            zz = sB("zz", [P, 2, S])
            y_t = sB("y_t", [P, 2, HALF])
            flag = sB("flag", [P, GROUPS * GROUPS])
            inv_win = sB("inv_win", [P, GROUPS])
            head_fix = sB("head_fix", [P, GROUPS * PAD])
            b_first = sB("b_first", [P, D])

        g_first = y_t[:, :, :].rearrange("p a b -> p (a b)")
        normed = [normed_out[:, t, :] for t in range(NC)]
        squares_a, squares_b = tmp_a[:, :], x_lo[:, 0, :]

        wide = pb("wide", [P, 4, HALF])
        ps_s = pb("ps_s", [P, HALF])
        ps_intra = pb("ps_intra", [P, HALF])
        ps_inter = pb("ps_inter", [P, HALF])
        ps_state = pb("ps_state", [P, HALF])

        par_rows = tmp_c[:, 0:2 * P].rearrange("p (b n) -> p b n", b=2)
        g_raw = tmp_a[:, :]
        g_hi, g_lo = y_hi[:, 0, :], y_lo[:, 0, :]
        HI, LF = slice(0, HEADS), slice(32, 32 + HEADS)
        rows = qT
        i_row, f_row = kT[HI, :], kT[LF, :]
        f_abs = tmp_c[LF, :]
        lf_row = tmp_c[HI, :]
        flat = num[:, :, :].rearrange("p c d -> p (c d)")
        bcum, m_row = flat[HI, 0:S], flat[HI, S:2 * S]
        carry, keep = xc[HI, 0, :], xc[HI, 1, :]
        m_prev, m_last = small[HI, 0, :], small[HI, 1, :]
        w_chunk = small[LF, 2, :]

        def by_chunk(row):
            return row.rearrange("p (c t) -> p c t", t=CHUNK)

        x_in = [sem("x_in0"), sem("x_in1")]
        const_set = sem("const_set")
        par_in = sem("par_in")
        rows_full = sem("rows_full")
        gw_in = sem("gw_in")
        gw_hi = sem("gw_hi")
        gw_lo = sem("gw_lo")
        raw_in = [sem("raw_in0"), sem("raw_in1")]
        hi_ready = sem("hi_ready")
        lo_ready = sem("lo_ready")
        wide_full = sem("wide_full")
        wide_taken = [sem(f"wide_taken{b}") for b in range(4)]
        xt_hi = sem("xt_hi")
        gate_act = sem("gate_act")
        gate_vec = sem("gate_vec")
        rows_out = sem("rows_out")
        m_in = sem("m_in")
        wc_in = sem("wc_in")
        qkv_in = sem("qkv_in")
        vec_step = sem("vec_step")
        conv_ready = sem("conv_ready")
        conv_tanh = sem("conv_tanh")
        z_tanh = sem("z_tanh")
        o_used = sem("o_used")
        xc_ready = sem("xc_ready")
        xc_high = sem("xc_high")
        xc_low = sem("xc_low")
        qkv_high = sem("qkv_high")
        qkv_low = sem("qkv_low")
        xm_high = sem("xm_high")
        xm_low = sem("xm_low")
        y_sum = sem("y_sum")
        y_rounded = sem("y_rounded")
        y_ready = sem("y_ready")
        dist_ready = sem("dist_ready")
        wgt_ready = sem("wgt_ready")
        s_full = sem("s_full")
        s_taken = sem("s_taken")
        num_full = sem("num_full")
        intra_taken = sem("intra_taken")
        state_ready = sem("state_ready")
        var_ready = sem("var_ready")
        rstd_ready = sem("rstd_ready")
        hn_ready = sem("hn_ready")
        ln_mean = sem("ln_mean")
        ln_squares = sem("ln_squares")
        ln_var = sem("ln_var")
        ln_rstd = sem("ln_rstd")
        ln_x = sem("ln_x")
        x1_hi = sem("x1_hi")
        x1_lo = [sem("x1_lo0"), sem("x1_lo1")]
        gb_in = sem("gb_in")
        acc_gain = sem("acc_gain")
        acc_ready = sem("acc_ready")
        pool_set = sem("pool_set")
        pool_sum = sem("pool_sum")
        pool_rounded = sem("pool_rounded")
        pool_ready = sem("pool_ready")
        ln_gain = sem("ln_gain")
        ln_scaled = sem("ln_scaled")
        ln_done = sem("ln_done")
        ln_done_late = sem("ln_done_late")
        stored = sem("stored")

        block = ctx.enter_context(nc.Block())

        def link(eng, ins, s, value):
            ins.then_inc(s, 1)
            eng.wait_ge(s, value)

        def link_taken(eng, ins, uses, k):
            link(eng, ins, wide_taken[k % 4], uses.taken(k))

        def wait_taken(eng, uses, k):
            eng.wait_ge(wide_taken[k % 4], uses.taken(k))

        def bank(k):
            return wide[:, k % 4, :]

        def half(n):
            return slice(n * HALF, (n + 1) * HALF)

        def tile(t):
            return slice(t * P, (t + 1) * P)

        def col(i):
            return cols[:, bass.ds(i, 1)]

        def slot_base(h):
            return 0 if isinstance(h, int) and h == 0 else h * SLOTS_PER_HEAD - 2

        @block.sync
        def _(sp):
            def load_x(m):
                for t in range(4 * m, 4 * m + 4):
                    sp.dma_start(acc[:, t, :], x[t * P:(t + 1) * P, :]).then_inc(x_in[m], 16)

            load_x(0)
            sp.wait_ge(const_set, SET_PAR)
            sp.dma_start(par_rows[0:COL_B, 0, :], conv_w.rearrange("k (t p) -> (k t) p", p=P)).then_inc(par_in, 16)
            for c, v in ((COL_B, conv_b), (COL_G, norm_g), (COL_SKIP, skip)):
                sp.dma_start(par_rows[c:c + ET, 0, :], v.rearrange("o (t p) -> (o t) p", p=P)).then_inc(par_in, 16)
            for c, v in ((COL_SCALE, p_scale), (COL_LNG, ln_g[0:1, :]), (COL_LNB, ln_b[0:1, :])):
                sp.dma_start(par_rows[c - P:c - P + v.shape[1] // P, 1, :],
                             v.rearrange("o (t p) -> (o t) p", p=P)).then_inc(par_in, 16)
            sp.wait_ge(const_set, SET_GATES)
            gw = w_in[:, 3 * E:3 * E + 2 * HEADS].rearrange("(k p) n -> p k n", p=P)
            gv = g_raw.rearrange("p (k n) -> p k n", k=KT)
            sp.dma_start(gv[:, :, HI], gw[:, :, 0:HEADS]).then_inc(gw_in, 16)
            sp.dma_start(gv[:, :, LF], gw[:, :, HEADS:2 * HEADS]).then_inc(gw_in, 16)
            sp.dma_start(bias[HI, :], b_i.rearrange("o h -> h o")).then_inc(gw_in, 16)
            sp.dma_start(bias[LF, :], b_f.rearrange("o h -> h o")).then_inc(gw_in, 16)

            def load_slot(s, k, src):
                if k is None:
                    k = s
                else:
                    sp.wait_ge(lo_ready, s - 1)
                dst = w_raw[:, k % 2, :].rearrange("p (k n) -> p k n", k=src.shape[1])
                sp.dma_start(dst, src).then_inc(raw_in[k % 2], 16)

            def in_cols(w, c):
                return w[:, bass.ds(c, P)].rearrange("(k p) n -> p k n", p=P)

            def out_rows(w, r, n):
                return w[bass.ds(r, 2 * P), half(n)].rearrange("(k p) n -> p k n", p=P)

            def load_qkv(h):
                for i, (w, n) in enumerate(((w_q, DK), (w_k, DK), (w_v, DV))):
                    sp.dma_start(w_qkv[:, i * 2 * DK:i * 2 * DK + 2 * n].rearrange("p (k n) -> p k n", k=2),
                                 w[bass.ds(h, 1), :, :].rearrange("o (k p) n -> p (o k) n", p=P)).then_inc(qkv_in, 16)

            load_slot(0, None, in_cols(w_in, 0))
            load_x(1)
            load_slot(1, None, in_cols(w_in, P))
            load_qkv(0)
            for j in range(2):
                load_slot(2 + j, j, in_cols(w_in, E + j * P))
            sp.wait_ge(gate_vec, VEC_M)
            sp.dma_start(m_rows, m_row).then_inc(rows_out, 16)
            sp.wait_ge(gate_act, ACT_EI)
            sp.dma_start(wc_rows, w_chunk).then_inc(rows_out, 16)
            sp.wait_ge(rows_out, 32)
            sp.dma_start(wc_bc[:, :], wc_rows.rearrange("h c -> (h c)").partition_broadcast(P)).then_inc(wc_in, 16)
            sp.dma_start(m_bc[:, :], m_rows[0, :].partition_broadcast(P)).then_inc(m_in, 16)
            for j in range(2):
                load_slot(4 + j, j, in_cols(w_in, 2 * E + j * P))

            with sp.Fori(1, HEADS) as h:
                s0 = slot_base(h)
                for j in range(2):
                    load_slot(s0 + j, j, in_cols(w_in, h * DV + j * P))
                sp.wait_ge(wide_full, head_uses(h).full(LATER["v"][3] - USES_PER_HEAD))
                load_qkv(h)
                for n in range(2):
                    load_slot(s0 + 2 + n, n, out_rows(w_out, h * DV - DV, n))
                for j in range(2):
                    load_slot(s0 + 4 + j, j, in_cols(w_in, h * DV + (E + j * P)))
                sp.wait_ge(dist_ready, h * NC)
                sp.dma_start(m_bc[:, :], m_rows[bass.ds(h, 1), :].rearrange("o t -> (o t)")
                             .partition_broadcast(P)).then_inc(m_in, 16)
                for j in range(2):
                    load_slot(s0 + 6 + j, j, in_cols(w_in, h * DV + (2 * E + j * P)))

            for n in range(2):
                load_slot(SLOT_LAST_OUT + n, n, out_rows(w_out, (HEADS - 1) * DV, n))
            sp.wait_ge(wide_full, BETWEEN.full(BRIDGE_T[-1]))
            sp.dma_start(g_first, ln_g[0, :].partition_broadcast(P)).then_inc(gb_in, 16)
            sp.dma_start(b_first[:, :], ln_b[0, :].partition_broadcast(P)).then_inc(gb_in, 16)

            def group_loads(g, last):
                s0 = g * SLOTS_PER_GROUP + SLOT_POOL
                for j in range(4):
                    load_slot(s0 + j, j, in_cols(p_in, g * CG + j * P))
                for p in range(2):
                    for j in range(2):
                        load_slot(s0 + GS_Z[p] + j, GS_Z[p] + j, in_cols(p_in, g * CG + (E + (2 * p + j) * P)))
                    if p == 1:
                        for n in range(2):
                            load_slot(s0 + GS_OUT[0] + n, GS_OUT[0] + n, out_rows(p_out, g * CG, n))
                        load_mix(g, s0, 1)
                        for n in range(2):
                            load_slot(s0 + GS_OUT[1] + n, GS_OUT[1] + n, out_rows(p_out, g * CG + 2 * P, n))
                    else:
                        load_mix(g, s0, 0)

            def load_mix(g, s0, p):
                load_slot(s0 + GS_MIX[p], GS_MIX[p], p_group[bass.ds(g, 1), :, p * 2 * P:(p + 1) * 2 * P]
                          .rearrange("o (k p) n -> p (o k) n", p=P))

            with sp.Fori(0, GROUPS - 1) as g:
                group_loads(g, False)
            group_loads(GROUPS - 1, True)
            sp.wait_ge(wide_full, group_uses(GROUPS - 1).full(G_MIX[1] + 3))
            sp.dma_start(g_bc[:, :], ln_g[1, :].partition_broadcast(P)).then_inc(gb_in, 16)
            sp.dma_start(b_bc[:, :], ln_b[1, :].partition_broadcast(P)).then_inc(gb_in, 16)
            for t in range(NC):
                if t < LATE:
                    sp.wait_ge(ln_done, t + 1)
                else:
                    sp.wait_ge(ln_done_late, t - LATE + 1)
                sp.dma_start(out[t * P:(t + 1) * P, :], normed[t]).then_inc(stored, 16)
            sp.wait_ge(stored, 16 * NC)

        @block.gpsimd
        def _(pool):
            sets = [
                lambda: pool.memset(ident[:, :], 0.0),
                lambda: pool.affine_select(out=ident[:, :], in_=ident[:, :], compare_op=ALU.not_equal, fill=1.0,
                                           base=0, pattern=[[-1, P]], channel_multiplier=1),
                lambda: pool.memset(par_rows, 0.0),
                lambda: pool.memset(g_raw, 0.0),
                lambda: pool.memset(mask[:, :], 0.0),
                lambda: pool.affine_select(out=mask[:, :], in_=mask[:, :], compare_op=ALU.is_ge, fill=FAR,
                                           base=0, pattern=[[1, P]], channel_multiplier=-1),
                lambda: pool.memset(rows[:, :], 0.0),
                lambda: pool.memset(keep, 1.0),
                lambda: pool.memset(by_chunk(keep)[:, :, 0:1], 0.0),
                lambda: pool.memset(carry, 0.0),
                lambda: pool.memset(small[:, :, :], 0.0),
                lambda: pool.memset(v_sb[:, :, DV:DV + 1], 1.0),
                lambda: pool.memset(xm[:, :, 0:HALO], 0.0),
                lambda: pool.memset(nhalf[:, :], -0.5),
            ]
            assert len(sets) == CONST_SETS
            for n, f in enumerate(sets):
                link(pool, f(), const_set, n + 1)

            def make_lo(s, k):
                pool.wait_ge(hi_ready, s + 1)
                link(pool, pool.tensor_tensor(w_lo[:, k % 2, :], w_raw[:, k % 2, :],
                                              w_hi[:, k % 2, :].bitcast(F32), ALU.subtract), lo_ready, s + 1)

            def power(ready, done, n, dst, src, k):
                pool.wait_ge(ready, n)
                link(pool, pool.tensor_tensor(dst, src, nhalf[:, 0:k], ALU.pow), done, n)

            def head(h, at):
                s0 = slot_base(h)
                for k in range(2, at["slots"]):
                    make_lo(s0 + k, k)
                    if k == 3:
                        pool.wait_ge(qkv_high, h + 1)
                        link(pool, pool.tensor_tensor(qkv_lo[:, :], w_qkv[:, :], qkv_hi[:, :].bitcast(F32),
                                                      ALU.subtract), qkv_low, h + 1)

                def powers(f):
                    part = slice(4 * f, 4 * f + 4)
                    power(var_ready, rstd_ready, h * 2 + (f + 1), rstd[:, part], small[:, 3, part], 4)

                powers(0)
                for f in range(2):
                    make_lo(s0 + (at["slots"] + f), f)
                powers(1)

            def deviation(t, n):
                pool.wait_ge(ln_squares, n + t + 1)
                link(pool, pool.tensor_scalar(small[:, 3, t:t + 1], small[:, 3, t:t + 1], 1.0 / D, EPS,
                                              ALU.mult, ALU.add), ln_var, n + t + 1)
                link(pool, pool.tensor_tensor(rstd[:, t:t + 1], small[:, 3, t:t + 1], nhalf[:, 0:1], ALU.pow),
                     ln_rstd, n + t + 1)

            make_lo(0, 0)
            make_lo(1, 1)
            head(0, FIRST)
            with pool.Fori(1, HEADS) as h:
                head(h, LATER)
            sets = [lambda part=part: pool.memset(part, 0.0)
                    for part in (u_buf[:, :, 0:PAD], win_a[:, 0:PAD], win_b[:, 0:PAD], flag[:, :])]
            for g, win in enumerate(WINDOWS):
                at = g * PAD
                for part, value in ((flag[:, g * GROUPS:g * GROUPS + g + 1], 1.0), (inv_win[:, g:g + 1], 1.0 / win),
                                    (head_fix[:, at:at + PAD], 1.0),
                                    *((head_fix[:, at + t:at + t + 1], win / (t + 1)) for t in range(win - 1))):
                    sets.append(lambda part=part, value=value: pool.memset(part, value))
            assert len(sets) == POOL_SETS

            def low_even(ns):
                for n in ns:
                    pool.wait_ge(x1_hi, n + 1)
                    dst = (slice(None), n % KT, half(n // KT))
                    link(pool, pool.tensor_tensor(x_lo[dst], x_new[:, n % 4, :], x_hi[dst].bitcast(F32),
                                                  ALU.subtract), x1_lo[0], n // 2 + 1)

            n = 0
            for t in range(6):
                deviation(t, 0)
                if t == 1:
                    pool.wait_ge(wide_full, BETWEEN.full(BRIDGE_T[-1]))
                if t >= 1:
                    for f in sets[(t - 1) * 9:t * 9]:
                        n += 1
                        link(pool, f(), pool_set, n)
            assert n == POOL_SETS
            low_even((0, 2))
            deviation(6, 0)
            low_even((4,))
            make_lo(SLOT_POOL, 0)
            low_even((6,))
            deviation(7, 0)
            make_lo(SLOT_POOL + 1, 1)
            low_even(range(8, 16, 2))
            shifts = {3: (0,), 4: (1,), 6: (2, 3), 7: (4, 5), 8: (6, 7)}
            for k in range(2, SLOTS_PER_GROUP + 2):
                make_lo(SLOT_POOL + k, k)
                for t in shifts.get(k, ()):
                    pool.wait_ge(acc_gain, t + 1)
                    link(pool, pool.tensor_tensor(acc[:, t, :], acc[:, t, :], b_first[:, :], ALU.add),
                         acc_ready, t + 1)
            with pool.Fori(1, GROUPS - 1) as g:
                s0 = g * SLOTS_PER_GROUP + SLOT_POOL
                for k in range(2, SLOTS_PER_GROUP + 2):
                    make_lo(s0 + k, k)
            s0 = (GROUPS - 1) * SLOTS_PER_GROUP + SLOT_POOL
            for k in range(2, SLOTS_PER_GROUP):
                make_lo(s0 + k, k)
            pool.wait_ge(gb_in, 64)
            for t in range(NC):
                deviation(t, NC)
                if 0 < t <= LATE:
                    pool.wait_ge(ln_scaled, t)
                    link(pool, pool.tensor_tensor(normed[t - 1], normed[t - 1], b_bc[:, :], ALU.add),
                         ln_done, t)

        @block.scalar
        def _(act):
            def make_hi(s, k):
                act.wait_ge(raw_in[k % 2], (s - k % 2) * 8 + 16)
                link(act, act.activation(w_hi[:, k % 2, :], w_raw[:, k % 2, :], ACT.Copy), hi_ready, s + 1)

            def take(uses, k, dst, scale=1.0):
                act.wait_ge(wide_full, uses.full(k))
                link_taken(act, act.activation(dst, bank(k), ACT.Copy, scale=scale), uses, k)

            def round_x(m):
                for n in range(KT * m, KT * m + KT):
                    k = USE_X[n]
                    act.wait_ge(wide_full, k + 1)
                    link(act, act.activation(x_hi[:, n % KT, half(m)], bank(k), ACT.Copy), xt_hi, n + 1)

            n = [0]

            def gate(ins):
                n[0] += 1
                link(act, ins, gate_act, n[0])

            def gate_rows(m):
                k = USE_GATES[m]
                act.wait_ge(wide_full, k + 1)
                gate(act.activation(i_row[:, half(m)], wide[HI, k % 4, :], ACT.Identity, bias=bias[HI, :]))
                link_taken(act, act.activation(f_row[:, half(m)], wide[LF, k % 4, :], ACT.Identity,
                                               bias=bias[LF, :]), START, k)

            round_x(0)
            act.wait_ge(gw_in, 64)
            link(act, act.activation(g_hi, g_raw, ACT.Copy), gw_hi, 1)
            make_hi(0, 0)
            gate_rows(0)
            round_x(1)
            make_hi(1, 1)
            gate_rows(1)
            gate(act.activation(f_abs, f_row, ACT.Abs))
            gate(act.activation(f_abs, f_abs, ACT.Exp, scale=-1.0))
            gate(act.activation(f_abs, f_abs, ACT.Ln, bias=1.0))
            assert n[0] == ACT_LN

            def gate_exponents():
                act.preload_act_table(ACT.Tanh)
                act.wait_ge(gate_vec, VEC_ROWS)
                gate(act.activation(rows[64:64 + HEADS, :], lf_row, ACT.Exp, scale=-1.0))
                yield
                for c in range(NC):
                    gate(act.activation(rows[LF, tile(c)], m_row[:, tile(c)], ACT.Exp, scale=-1.0,
                                        bias=m_prev[:, c:c + 1]))
                gate(act.activation(w_chunk, by_chunk(rows[LF, :])[:, :, CHUNK - 1], ACT.Copy))
                assert n[0] == ACT_EI
                for c in range(NC):
                    gate(act.activation(rows[96:96 + HEADS, tile(c)], rows[HI, tile(c)], ACT.Exp,
                                        bias=m_last[:, c:c + 1]))
                assert n[0] == ACT_ROWS

            def round_y(n, m, src):
                link(act, act.activation(y_hi[:, m % 2, half(m // 2)], src, ACT.Copy), y_rounded, n)

            def prev_y(h, ms):
                for m in ms:
                    act.wait_ge(y_sum, h * 4 + (m + 1))
                    round_y(h * 4 + (m + 1), m, tmp_c[:, half(m % 2)])

            def head(h, at, first):
                uses, s0 = head_uses(h), slot_base(h)
                for j in range(2):
                    for n in range(2):
                        k = at["xm"][j] + n
                        take(uses, k, xm[:, j, HALO + n * HALF:HALO + (n + 1) * HALF])
                        if j == 0 and n == 1:
                            make_hi(s0 + 2, 0)
                            if not first:
                                prev_y(h - 1, range(3))
                        if j == 1 and n == 0 and not first:
                            prev_y(h - 1, range(3, 4))
                make_hi(s0 + 3, 1)
                act.wait_ge(qkv_in, h * 48 + 48)
                link(act, act.activation(qkv_hi[:, :], w_qkv[:, :], ACT.Copy), qkv_high, h + 1)
                exponents = gate_exponents() if first else None
                if first:
                    next(exponents)

                def round_xc(j):
                    act.wait_ge(xc_ready, h * 2 + (j + 1))
                    link(act, act.activation(xc_hi[:, j, :], xc[:, j, :], ACT.Copy), xc_high, h * 2 + (j + 1))

                def round_xm(n):
                    link(act, act.activation(xm_hi[:, :, :], xm[:, :, HALO + n * HALF:HALO + (n + 1) * HALF],
                                             ACT.Copy), xm_high, h * 2 + (n + 1))

                def take_v(n):
                    k = at["v"][n]
                    act.wait_ge(wide_full, uses.full(k))
                    link_taken(act, act.activation(v_sb[:, 2 * n:2 * n + 2, 0:DV],
                                                   bank(k).rearrange("p (t d) -> p t d", t=2), ACT.Copy), uses, k)

                def conv_gate(j):
                    act.wait_ge(conv_ready, h * 2 + (j + 1))
                    link(act, act.activation(tmp_c[:, :], tmp_a[:, :], ACT.Tanh), conv_tanh, h * 2 + (j + 1))

                conv_gate(0)
                if first:
                    next(exponents, None)
                    act.wait_ge(rows_out, 32)
                if not first:
                    for n in range(2):
                        act.wait_ge(wide_full, uses.full(at["out"] + NC * (n + 1) - 1))
                        make_hi(s0 + (4 + n), n)
                conv_gate(1)
                for m in range(4):
                    k = at["z"] + m
                    act.wait_ge(wide_full, uses.full(k))
                    if m >= 2:
                        wait_taken(act, uses, k - 2)
                    link(act, act.activation(gate_t[:, m % 2, :], bank(k), ACT.Tanh, scale=0.5),
                         z_tanh, h * 4 + (m + 1))
                    if m % 2:
                        make_hi(s0 + (at["s_o"] + m // 2), m // 2)
                    if m < 2:
                        round_xc(m)
                    elif m == 2:
                        round_xm(0)
                for n in range(2):
                    take(uses, at["q"] + n, qT[:, half(n)], DK ** -0.5)
                take_v(0)
                act.wait_ge(wide_full, uses.full(at["v"][1]))
                round_xm(1)
                take_v(1)
                for n in range(2):
                    take(uses, at["k"] + n, kT[:, half(n)])
                for n in range(2, 4):
                    take_v(n)

                def decay(c):
                    act.wait_ge(dist_ready, h * NC + (c + 1))
                    link(act, act.activation(wgt[:, :], dist[:, :], ACT.Exp, scale=-1.0),
                         wgt_ready, h * NC + (c + 1))

                decay(0)
                for c in range(NC):
                    if c + 1 < NC:
                        decay(c + 1)
                    act.wait_ge(num_full, h * NC + (c + 1))
                    link(act, act.activation(num[:, c, :], ps_intra[:, 0:DV + 1], ACT.Copy),
                         intra_taken, h * NC + (c + 1))
                    if c % 2:
                        m = c // 2
                        k = at["o"] + m
                        act.wait_ge(wide_full, uses.full(k))
                        if m >= 2:
                            act.wait_ge(o_used, h * 4 + (m - 1))
                        link_taken(act, act.activation(gate_t[:, m % 2, :], bank(k), ACT.Tanh, scale=0.5), uses, k)
                        if m % 2:
                            make_hi(s0 + (at["slots"] + m // 2), m // 2)

            head(0, FIRST, True)
            with act.Fori(1, HEADS) as h:
                head(h, LATER, False)
            prev_y(HEADS - 1, range(2))

            def sum_squares(t, n, squares):
                act.wait_ge(ln_mean, n + t + 1)
                link(act, act.activation(squares, acc[:, t, :], ACT.Square, bias=small[:, 2, t:t + 1],
                                         accum_out=small[:, 3, t:t + 1]), ln_squares, n + t + 1)

            def form_x(n):
                k, t = BRIDGE_X[n], n % KT
                if n >= 4:
                    act.wait_ge(x1_lo[0], (n - 4) // 2 + 1)
                act.wait_ge(wide_full, BETWEEN.full(k))
                link_taken(act, act.activation(x_new[:, n % 4, :], bank(k), ACT.Identity,
                                               scale=cols[:, COL_LNG + t:COL_LNG + t + 1],
                                               bias=cols[:, COL_LNB + t:COL_LNB + t + 1]), BETWEEN, k)

            def next_input(ns):
                for n in ns:
                    if n % 2:
                        wait_taken(act, BETWEEN, BRIDGE_X[n])
                    else:
                        form_x(n)
                    link(act, act.activation(x_hi[:, n % KT, half(n // KT)], x_new[:, n % 4, :], ACT.Copy),
                         x1_hi, n + 1)

            for t in range(6):
                sum_squares(t, 0, squares_a)
                if t == 1:
                    prev_y(HEADS - 1, range(2, 4))
            next_input(range(3))
            sum_squares(6, 0, squares_a)
            next_input(range(3, 6))
            act.wait_ge(wide_full, BETWEEN.full(BRIDGE_O[-1]))
            make_hi(SLOT_POOL, 0)
            next_input(range(6, 7))
            sum_squares(7, 0, squares_a)
            next_input(range(7, 8))
            make_hi(SLOT_POOL + 1, 1)
            act.wait_ge(pool_set, POOL_SETS)

            def group(g, first, last):
                uses, s0 = group_uses(g), g * SLOTS_PER_GROUP + SLOT_POOL

                def next_hi(k):
                    if k + 2 < SLOTS_PER_GROUP or not last:
                        make_hi(s0 + (k + 2), k)

                def round_pooled(j):
                    act.wait_ge(pool_sum, g * 4 + (j + 1))
                    link(act, act.activation(p_hi[:, j, :], win_a[:, PAD:PAD + S], ACT.Copy),
                         pool_rounded, g * 4 + (j + 1))

                def take_u(j, n):
                    take(uses, G_U + 2 * j + n, u_buf[:, j % 2, PAD + n * HALF:PAD + (n + 1) * HALF])

                def z_gate(p):
                    for m in range(4):
                        k = G_Z[p] + m
                        act.wait_ge(wide_full, uses.full(k))
                        if m >= 2:
                            wait_taken(act, uses, k - 2)
                        link(act, act.activation(gate_t[:, m % 2, :], bank(k), ACT.Tanh, scale=0.5),
                             z_tanh, g * 8 + (4 * HEADS + 4 * p + m + 1))
                        if p == 0 and m == 0:
                            round_pooled(3)
                        if m % 2:
                            next_hi(GS_Z[p] + m // 2)

                def mixed(p):
                    for m in range(4):
                        if m == 3:
                            act.wait_ge(wide_full, uses.full(G_MIX[p] + m))
                            next_hi(GS_MIX[p])
                        wait_taken(act, uses, G_MIX[p] + m)
                        round_y(g * 8 + (4 * HEADS + 4 * p + m + 1), m, y_t[:, m % 2, :])

                def projected(p):
                    for n in range(2):
                        act.wait_ge(wide_full, uses.full(G_OUT[p] + NC * (n + 1) - 1))
                        next_hi(GS_OUT[p] + n)

                if first:
                    for j, ns in enumerate((range(8, 11), range(11, 16))):
                        take(BETWEEN, BRIDGE_U[j], u_buf[:, j, PAD:PAD + HALF])
                        next_input(ns)
                    for part_lo in x1_lo:
                        act.wait_ge(part_lo, KT)
                    for j in range(2):
                        take(uses, 2 + j, u_buf[:, j, PAD + HALF:PAD + S])
                        next_hi(GS_U + j)
                    round_pooled(0)
                for j in range(2 if first else 0, 4):
                    take_u(j, 0)
                    if j:
                        round_pooled(j - 1)
                    take_u(j, 1)
                    next_hi(GS_U + j)
                z_gate(0)
                mixed(0)
                z_gate(1)
                projected(0)
                mixed(1)
                if not last:
                    projected(1)

            group(0, True, False)
            with act.Fori(1, GROUPS - 1) as g:
                group(g, False, False)
            group(GROUPS - 1, False, True)
            for t in range(NC):
                sum_squares(t, NC, squares_b)
                if t < LATE:
                    act.wait_ge(ln_gain, t + 1)
                    act.wait_ge(ln_rstd, NC + t + 1)
                    link(act, act.activation(normed[t], normed[t], ACT.Copy, scale=rstd[:, t:t + 1]),
                         ln_scaled, t + 1)

        @block.vector
        def _(dve):
            base, steps = [0], [0]

            def step(ins, wait=True):
                steps[0] += 1
                ins.then_inc(vec_step, 1)
                if wait:
                    dve.wait_ge(vec_step, base[0] + steps[0])

            def part(start, count, f):
                base[0], steps[0] = start, 0
                f()
                assert steps[0] == count, (steps[0], count)

            def residual(uses, k, t, n):
                dve.wait_ge(wide_full, uses.full(k))
                link_taken(dve, dve.tensor_tensor(acc[:, t, half(n)], bank(k), acc[:, t, half(n)], ALU.add), uses, k)

            def start():
                def low_x(m):
                    for n in range(KT * m, KT * m + KT):
                        k = USE_X[n]
                        dve.wait_ge(xt_hi, n + 1)
                        link_taken(dve, dve.tensor_tensor(x_lo[:, n % KT, half(m)], bank(k),
                                                          x_hi[:, n % KT, half(m)].bitcast(F32), ALU.subtract),
                                   START, k)

                low_x(0)
                dve.wait_ge(wide_full, USE_PAR[1] + 1)
                link_taken(dve, dve.tensor_copy(cols[:, 0:P], bank(USE_PAR[0])[:, 0:P]), START, USE_PAR[0])
                link_taken(dve, dve.tensor_copy(cols[:, P:COLS], bank(USE_PAR[1])[:, 0:COLS - P]), START, USE_PAR[1])
                dve.wait_ge(gw_hi, 1)
                link(dve, dve.tensor_tensor(g_lo, g_raw, g_hi.bitcast(F32), ALU.subtract), gw_lo, 1)
                low_x(1)
                for a, b, f in ((COL_W, COL_G, 0.5), (COL_G, COL_SKIP, 0.25), (COL_SKIP, COL_SCALE, 0.5),
                                (COL_SCALE, COL_LNG, 0.5)):
                    step(dve.tensor_scalar(cols[:, a:b], cols[:, a:b], f, None, ALU.mult))
                dve.wait_ge(const_set, CONST_SETS)
                dve.wait_ge(gate_act, ACT_LN)
                n = 0

                def gate(ins):
                    nonlocal n
                    n += 1
                    link(dve, ins, gate_vec, n)

                gate(dve.scalar_tensor_tensor(out=lf_row, in0=f_row, scalar=0.0, in1=f_abs,
                                              op0=ALU.min, op1=ALU.subtract))
                gate(dve.tensor_tensor_scan(bcum, keep, lf_row, 0.0, ALU.mult, ALU.add))
                gate(dve.tensor_tensor(rows[HI, :], i_row, bcum, ALU.subtract))
                gate(dve.tensor_copy(by_chunk(carry)[:, 1:NC, 0], by_chunk(bcum)[:, 0:NC - 1, CHUNK - 1]))
                gate(dve.tensor_tensor_scan(m_row, carry, rows[HI, :], 0.0, ALU.add, ALU.max))
                assert n == VEC_M
                gate(dve.tensor_tensor(m_prev[:, 1:NC], by_chunk(m_row)[:, 0:NC - 1, CHUNK - 1],
                                       by_chunk(bcum)[:, 0:NC - 1, CHUNK - 1], ALU.add))
                gate(dve.tensor_scalar(m_last, by_chunk(m_row)[:, :, CHUNK - 1], -1.0, None, ALU.mult))
                assert n == VEC_PREV
                gate(dve.tensor_tensor(lf_row, bcum, m_row, ALU.add))
                assert n == VEC_ROWS
            part(0, VEC_START, start)

            def gated_output(h, uses, at, ms=range(4)):
                def summed(m):
                    k, j, n = at[m], m % 2, m // 2
                    dve.wait_ge(wide_full, uses.full(k))
                    link_taken(dve, dve.scalar_tensor_tensor(
                        out=tmp_c[:, half(m % 2)], in0=bank(k), scalar=col(h * 2 + (COL_G + j)),
                        in1=e_buf[:, j, half(n)], op0=ALU.mult, op1=ALU.mult), uses, k)
                    link(dve, dve.tensor_tensor(tmp_c[:, half(m % 2)], tmp_c[:, half(m % 2)],
                                                f_buf[:, j, half(n)], ALU.add), y_sum, h * 4 + (m + 1))

                for m in range(ms[0], ms[-1] + 2):
                    if m in ms:
                        summed(m)
                    if m - 1 in ms:
                        lo_part(h * 4 + m, m - 1, tmp_c[:, half((m - 1) % 2)])

            def lo_part(n, m, src):
                dve.wait_ge(y_rounded, n)
                dst = (slice(None), m % 2, half(m // 2))
                link(dve, dve.tensor_tensor(y_lo[dst], src, y_hi[dst].bitcast(F32), ALU.subtract), y_ready, n)

            def head(h, at, first, last=False):
                uses = head_uses(h)

                def conv(j):
                    def tap(i):
                        if i == 0:
                            for n in range(2):
                                wait_taken(dve, uses, at["xm"][j] + n)
                            step(dve.tensor_scalar(tmp_a[:, :], xm[:, j, HALO:HALO + S],
                                                   col(h * 2 + (COL_W + 3 * ET + j)), col(h * 2 + (COL_B + j)),
                                                   ALU.mult, ALU.add))
                            return
                        w = HALO - i
                        ins = dve.scalar_tensor_tensor(
                            out=tmp_a[:, :], in0=xm[:, j, w:w + S], scalar=col(h * 2 + (COL_W + w * ET + j)),
                            in1=tmp_a[:, :], op0=ALU.mult, op1=ALU.add)
                        if i < HALO:
                            step(ins)
                        else:
                            link(dve, ins, conv_ready, h * 2 + (j + 1))

                    def gate():
                        dve.wait_ge(conv_tanh, h * 2 + (j + 1))
                        link(dve, dve.scalar_tensor_tensor(out=xc[:, j, :], in0=tmp_c[:, :], scalar=1.0,
                                                           in1=tmp_a[:, :], op0=ALU.add, op1=ALU.mult),
                             xc_ready, h * 2 + (j + 1))
                    return [lambda i=i: tap(i) for i in range(CONV)] + [gate]

                work = conv(0) + conv(1)
                if first:
                    for f in work:
                        f()
                else:
                    gated_output(h - 1, uses, [at["hn"] + m for m in range(4)])
                    for n in range(2):
                        for t in range(NC):
                            residual(uses, at["out"] + n * NC + t, t, n)
                            if t % 2 and len(work) > 2:
                                work.pop(0)()
                    for f in work:
                        f()
                def low_xm(n):
                    dve.wait_ge(xm_high, h * 2 + (n + 1))
                    link(dve, dve.tensor_tensor(xm_lo[:, :, :], xm[:, :, HALO + n * HALF:HALO + (n + 1) * HALF],
                                                xm_hi[:, :, :].bitcast(F32), ALU.subtract),
                         xm_low, h * 2 + (n + 1))

                for m in range(4):
                    k, j, n = at["z"] + m, m // 2, m % 2
                    dve.wait_ge(z_tanh, h * 4 + (m + 1))
                    link_taken(dve, dve.scalar_tensor_tensor(
                        out=e_buf[:, j, half(n)], in0=gate_t[:, m % 2, :], scalar=1.0, in1=bank(k),
                        op0=ALU.add, op1=ALU.mult), uses, k)
                    if n:
                        step(dve.tensor_tensor(f_buf[:, j, :], f_buf[:, j, :], e_buf[:, j, :], ALU.mult))
                    else:
                        step(dve.tensor_scalar(f_buf[:, j, :], xc[:, j, :], col(h * 2 + (COL_SKIP + j)), None, ALU.mult))
                        dve.wait_ge(xc_high, h * 2 + (j + 1))
                        link(dve, dve.tensor_tensor(xc_lo[:, j, :], xc[:, j, :], xc_hi[:, j, :].bitcast(F32),
                                                    ALU.subtract), xc_low, h * 2 + (j + 1))
                    if m == 2:
                        low_xm(0)
                step(dve.memset(state[:, :], 0.0))
                low_xm(1)

                def gate_col(c, q):
                    return gcol[:, c, q, bass.ds(h, 1)]

                def distance(c):
                    link(dve, dve.scalar_tensor_tensor(out=dist[:, :], in0=m_bc[:, tile(c)], scalar=gate_col(c, 0),
                                                       in1=mask[:, :], op0=ALU.subtract, op1=ALU.add),
                         dist_ready, h * NC + (c + 1))

                def weighted(c):
                    dve.wait_ge(s_full, h * NC + (c + 1))
                    dve.wait_ge(wgt_ready, h * NC + (c + 1))
                    step(dve.tensor_tensor(sT[:, :], ps_s[:, 0:P], wgt[:, :], ALU.mult))
                    link(dve, dve.tensor_scalar(kw[:, :], ps_s[:, P:2 * P], gate_col(c, 3), None, ALU.mult),
                         s_taken, h * NC + (c + 1))

                def scales(f):
                    part = slice(4 * f, 4 * f + 4)
                    big, r, r2, var = (small[:, i, part] for i in range(4))
                    step(dve.scalar_tensor_tensor(out=big, in0=num[:, part, DV], scalar=-1.0,
                                                  in1=gcol[:, part, 2, bass.ds(h, 1)].rearrange("p c o -> p (c o)"),
                                                  op0=ALU.mult, op1=ALU.max), wait=False)
                    for c in range(4 * f, 4 * f + 4):
                        step(dve.bn_aggr(mv[:, c, :], stats[:, c, :]), wait=c == 4 * f + 3)
                    step(dve.tensor_tensor(big, num[:, part, DV], big, ALU.max))
                    step(dve.reciprocal(r, big))
                    step(dve.tensor_tensor(r2, r, r, ALU.mult))
                    step(dve.tensor_tensor(var, r2, mv[:, part, 1], ALU.mult))
                    link(dve, dve.tensor_scalar(var, var, EPS, None, ALU.add), var_ready, h * 2 + (f + 1))

                def norm(f):
                    part = slice(4 * f, 4 * f + 4)
                    dve.wait_ge(rstd_ready, h * 2 + (f + 1))
                    step(dve.tensor_tensor(small[:, 2, part], small[:, 1, part], rstd[:, part], ALU.mult))
                    for c in range(4 * f, 4 * f + 4):
                        ins = dve.tensor_scalar(num[:, c, 0:DV], num[:, c, 0:DV], mv[:, c, 0:1],
                                                small[:, 2, c:c + 1], ALU.subtract, ALU.mult)
                        if c % 4 == 3:
                            link(dve, ins, hn_ready, h * 2 + (f + 1))
                        else:
                            step(ins)

                if first:
                    dve.wait_ge(rows_full, 1)
                    for m, ps in enumerate((ps_intra, ps_inter)):
                        step(dve.tensor_copy(gcol[:, 4 * m:4 * m + 4, :, :],
                                             ps[:, :].rearrange("p (c q r) -> p c q r", c=4, q=4)[:, :, :, 0:HEADS]))
                    dve.wait_ge(wc_in, 16)
                dve.wait_ge(m_in, h * 16 + 16)
                distance(0)
                weighted(0)
                distance(1)
                for c in range(NC):
                    dve.wait_ge(num_full, h * NC + (c + 1))
                    link(dve, dve.scalar_tensor_tensor(out=state[:, :], in0=state[:, :],
                                                       scalar=wc_bc[:, bass.ds(h * NC + c, 1)],
                                                       in1=ps_state[:, 0:DV + 1], op0=ALU.mult, op1=ALU.add),
                         state_ready, h * NC + (c + 1))
                    dve.wait_ge(intra_taken, h * NC + (c + 1))
                    step(dve.scalar_tensor_tensor(out=num[:, c, :], in0=ps_inter[:, 0:DV + 1], scalar=gate_col(c, 1),
                                                  in1=num[:, c, :], op0=ALU.mult, op1=ALU.add))
                    if c + 1 < NC:
                        weighted(c + 1)
                    if c + 2 < NC:
                        distance(c + 2)
                    if first:
                        step(dve.tensor_scalar(acc[:, c, :], acc[:, c, :], ALPHA, None, ALU.mult))
                    step(dve.bn_stats(stats[:, c, :], num[:, c, 0:DV]))
                    if c % 2:
                        m = c // 2
                        wait_taken(dve, uses, at["o"] + m)
                        j, n = m // 2, m % 2
                        link(dve, dve.scalar_tensor_tensor(out=e_buf[:, j, half(n)], in0=gate_t[:, m % 2, :],
                                                           scalar=1.0, in1=e_buf[:, j, half(n)],
                                                           op0=ALU.add, op1=ALU.mult), o_used, h * 4 + (m + 1))
                    if c == 4:
                        scales(0)
                    if c == 6:
                        norm(0)
                if last:
                    gated_output(h, BETWEEN, BRIDGE_T, range(2))
                scales(1)
                norm(1)

            part(VEC_START, VEC_FIRST, lambda: head(0, FIRST, True))
            with dve.Fori(1, HEADS - 1) as h:
                part(h * VEC_LATER + (VEC_START + VEC_FIRST - VEC_LATER), VEC_LATER, lambda: head(h, LATER, False))
            part(VEC_START + VEC_FIRST + (HEADS - 2) * VEC_LATER, VEC_LATER,
                 lambda: head(HEADS - 1, LATER, False, True))

            def residual_sum(uses, k, t, n):
                dve.wait_ge(wide_full, uses.full(k))
                link_taken(dve, dve.scalar_tensor_tensor(out=acc[:, t, half(n)], in0=bank(k), scalar=1.0,
                                                         in1=acc[:, t, half(n)], op0=ALU.mult, op1=ALU.add,
                                                         accum_out=small[:, n, t:t + 1]), uses, k)

            def mean(t, n):
                link(dve, dve.tensor_scalar(small[:, 2, t:t + 1], small[:, 0, t:t + 1], small[:, 1, t:t + 1],
                                            -1.0 / D, ALU.add, ALU.mult), ln_mean, n + t + 1)

            def between():
                def residual_tile(t):
                    if t < NC:
                        for n in range(2):
                            residual_sum(BETWEEN, BRIDGE_O[2 * t + n], t, n)
                        mean(t, 0)
                    if t:
                        dve.wait_ge(ln_rstd, t)
                        link(dve, dve.tensor_scalar(acc[:, t - 1, :], acc[:, t - 1, :], small[:, 2, t - 1:t],
                                                    rstd[:, t - 1:t], ALU.add, ALU.mult), ln_x, t)

                def form_x(n):
                    k, t = BRIDGE_X[n], n % KT
                    dve.wait_ge(wide_full, BETWEEN.full(k))
                    link_taken(dve, dve.tensor_scalar(x_new[:, n % 4, :], bank(k), cols[:, COL_LNG + t:COL_LNG + t + 1],
                                                      cols[:, COL_LNB + t:COL_LNB + t + 1], ALU.mult, ALU.add),
                               BETWEEN, k)

                def low_odd(n):
                    dve.wait_ge(x1_hi, n + 1)
                    dst = (slice(None), n % KT, half(n // KT))
                    link(dve, dve.tensor_tensor(x_lo[dst], x_new[:, n % 4, :], x_hi[dst].bitcast(F32),
                                                ALU.subtract), x1_lo[1], n // 2 + 1)

                for t in range(6):
                    residual_tile(t)
                    if t == 1:
                        gated_output(HEADS - 1, BETWEEN, BRIDGE_T, range(2, 4))
                form_x(1)
                low_odd(1)
                residual_tile(6)
                form_x(3)
                form_x(5)
                low_odd(3)
                low_odd(5)
                residual_tile(7)
                form_x(7)
                low_odd(7)
                residual_tile(8)
                for n in range(9, 16, 2):
                    form_x(n)
                    low_odd(n)
                dve.wait_ge(gb_in, 32)
                for v in (g_first, b_first[:, :]):
                    step(dve.tensor_scalar(v, v, ALPHA, None, ALU.mult))
                dve.wait_ge(pool_set, POOL_SETS)

            at_pool = VEC_START + VEC_FIRST + (HEADS - 1) * VEC_LATER
            part(at_pool, VEC_BETWEEN, between)

            def group(g, first, last):
                uses = group_uses(g)

                def gain(t):
                    link(dve, dve.tensor_tensor(acc[:, t, :], acc[:, t, :], g_first, ALU.mult), acc_gain, t + 1)

                for j in range(4):
                    if first and j < 2:
                        wait_taken(dve, uses, 2 + j)
                    else:
                        for n in range(2):
                            wait_taken(dve, uses, G_U + 2 * j + n)
                    src = u_buf[:, j % 2, :]
                    for level, dst in enumerate((win_a, win_b, win_a, win_b)):
                        back = PAD - (1 << level)
                        step(dve.scalar_tensor_tensor(out=dst[:, PAD:PAD + S], in0=src[:, back:back + S],
                                                      scalar=flag[:, bass.ds(g * GROUPS + level, 1)],
                                                      in1=src[:, PAD:PAD + S], op0=ALU.mult, op1=ALU.add))
                        src = dst
                    step(dve.tensor_tensor(win_b[:, PAD:2 * PAD], win_b[:, PAD:2 * PAD],
                                           head_fix[:, bass.ds(g * PAD, PAD)], ALU.mult))
                    link(dve, dve.scalar_tensor_tensor(out=win_a[:, PAD:PAD + S], in0=win_b[:, PAD:PAD + S],
                                                       scalar=inv_win[:, bass.ds(g, 1)],
                                                       in1=u_buf[:, j % 2, PAD:PAD + S],
                                                       op0=ALU.mult, op1=ALU.subtract), pool_sum, g * 4 + (j + 1))
                    dve.wait_ge(pool_rounded, g * 4 + (j + 1))
                    link(dve, dve.tensor_tensor(p_lo[:, j, :], win_a[:, PAD:PAD + S], p_hi[:, j, :].bitcast(F32),
                                                ALU.subtract), pool_ready, g * 4 + (j + 1))
                    if first and j < 2:
                        gain(j)

                def z_gate(p):
                    for m in range(4):
                        k = G_Z[p] + m
                        dve.wait_ge(z_tanh, g * 8 + (4 * HEADS + 4 * p + m + 1))
                        link_taken(dve, dve.scalar_tensor_tensor(
                            out=zz[:, m // 2, half(m % 2)], in0=gate_t[:, m % 2, :], scalar=1.0, in1=bank(k),
                            op0=ALU.add, op1=ALU.mult), uses, k)
                        if first and p == 0:
                            for t in ((2, 3), (4, 5), (6,), (7,))[m]:
                                gain(t)

                def mixed(p):
                    for m in range(5):
                        if m < 4:
                            k = G_MIX[p] + m
                            dve.wait_ge(wide_full, uses.full(k))
                            link_taken(dve, dve.scalar_tensor_tensor(
                                out=y_t[:, m % 2, :], in0=bank(k), scalar=col(g * 4 + (COL_SCALE + 2 * p + m % 2)),
                                in1=zz[:, m % 2, half(m // 2)], op0=ALU.mult, op1=ALU.mult), uses, k)
                        if m:
                            lo_part(g * 8 + (4 * HEADS + 4 * p + m), m - 1, y_t[:, (m - 1) % 2, :])

                def project(p):
                    for n in range(2):
                        for t in range(NC):
                            residual(uses, G_OUT[p] + n * NC + t, t, n)

                z_gate(0)
                mixed(0)
                z_gate(1)
                if first:
                    dve.wait_ge(acc_ready, NC)
                project(0)
                mixed(1)
                if not last:
                    project(1)
                    return
                dve.wait_ge(gb_in, 64)
                for i, (t, n) in enumerate(LAST_PROJECT):
                    residual_sum(uses, G_OUT[1] + i, t, n)
                    if n:
                        mean(t, NC)
                        link(dve, dve.scalar_tensor_tensor(out=normed[t], in0=acc[:, t, :], scalar=small[:, 2, t:t + 1],
                                                           in1=g_bc[:, :], op0=ALU.add, op1=ALU.mult), ln_gain, t + 1)
                for t in range(LATE, NC):
                    dve.wait_ge(ln_rstd, NC + t + 1)
                    link(dve, dve.scalar_tensor_tensor(out=normed[t], in0=normed[t], scalar=rstd[:, t:t + 1],
                                                       in1=b_bc[:, :], op0=ALU.mult, op1=ALU.add),
                         ln_done_late, t - LATE + 1)

            at_pool += VEC_BETWEEN
            part(at_pool, VEC_GROUP, lambda: group(0, True, False))
            with dve.Fori(1, GROUPS - 1) as g:
                part(g * VEC_GROUP + at_pool, VEC_GROUP, lambda: group(g, False, False))
            part(at_pool + (GROUPS - 1) * VEC_GROUP, VEC_GROUP, lambda: group(GROUPS - 1, False, True))

        @block.tensor
        def _(pe):
            def free(uses, k):
                if uses is not START or k >= 4:
                    pe.wait_ge(wide_taken[k % 4], uses.taken(k - 4))

            def split(dst, a, b, first, last):
                pe.matmul(dst, a[0], b[0], start=first, stop=False)
                pe.matmul(dst, a[0], b[1], start=False, stop=False)
                return pe.matmul(dst, a[1], b[0], start=False, stop=last)

            def in_product(uses, k, n, w, between=None):
                free(uses, k)
                for t in range(KT):
                    mm = split(bank(k), [v[:, tile(t)] for v in w], [v[:, t, half(n)] for v in (x_hi, x_lo)],
                               t == 0, t == KT - 1)
                    if t == KT - 1:
                        mm.then_inc(wide_full, 1)
                    if between and t % 4 == 3:
                        between()

            def slot(s0, k):
                pe.wait_ge(lo_ready, s0 + (k + 1))
                return w_hi[:, k % 2, :], w_lo[:, k % 2, :]

            def in_slot(uses, s0, ks, k, between=None):
                w = slot(s0, ks)
                for n in range(2):
                    in_product(uses, k + n, n, w, between)

            def out_product(uses, k, w, t):
                free(uses, k)
                for j in range(2):
                    mm = split(bank(k), [v[:, j, tile(t)] for v in (y_hi, y_lo)],
                               [v[:, half(j)] for v in w], j == 0, j == 1)
                mm.then_inc(wide_full, 1)

            def wait_y(n, t):
                if t % 4 == 0:
                    pe.wait_ge(y_ready, n + 2 + t // 2)

            def project(uses, k, s0, ks, y_before):
                for n in range(2):
                    w = slot(s0, ks + n)
                    for t in range(NC):
                        if n == 0:
                            wait_y(y_before, t)
                        out_product(uses, k + n * NC + t, w, t)

            def project_by_token(uses, k, s0, ks, y_before):
                ws = {}
                for i, (t, n) in enumerate(LAST_PROJECT):
                    if n not in ws:
                        ws[n] = slot(s0, ks + n)
                    if n == 0:
                        wait_y(y_before, t)
                    out_product(uses, k + i, ws[n], t)

            def turn(uses, k, srcs):
                free(uses, k)
                for i, src in enumerate(srcs):
                    mm = pe.transpose(bank(k)[:, tile(i)], src, ident[:, :])
                mm.then_inc(wide_full, 1)

            def x_turns(m):
                pe.wait_ge(x_in[m], 16 * 4)
                for t in range(KT):
                    turn(START, USE_X[KT * m + t], [acc[:, 4 * m + i, tile(t)] for i in range(4)])

            pe.wait_ge(const_set, SET_IDENT)
            x_turns(0)
            pe.wait_ge(par_in, 16 * 7)
            for b in range(2):
                turn(START, USE_PAR[b], [par_rows[:, b, :]])
            pe.wait_ge(gw_lo, 1)
            in_product(START, USE_GATES[0], 0, (g_hi, g_lo))
            x_turns(1)
            for k in USE_X[-4:]:
                wait_taken(pe, START, k)
            in_product(START, USE_GATES[1], 1, (g_hi, g_lo))

            def turn_hn(h, uses, at, ms=range(4)):
                for m in ms:
                    if m % 2 == 0:
                        pe.wait_ge(hn_ready, h * 2 + (m // 2 + 1))
                    turn(uses, at[m], [num[:, 4 * (m // 2) + i, (m % 2) * P:(m % 2 + 1) * P] for i in range(4)])

            def head(h, at, first):
                uses, s0 = head_uses(h), slot_base(h)
                in_slot(uses, s0, 0, at["xm"][0])
                if not first:
                    turn_hn(h - 1, uses, [at["hn"] + m for m in range(4)])
                in_slot(uses, s0, 1, at["xm"][1])
                if not first:
                    project(uses, at["out"], s0, at["s_out"], h * 4 - 4)
                for j in range(2):
                    in_slot(uses, s0, at["s_z"] + j, at["z"] + 2 * j)
                if first:
                    pe.wait_ge(gate_act, ACT_ROWS)
                    for c in range(NC):
                        mm = pe.transpose((ps_intra, ps_inter)[c // 4][:, tile(c % 4)], rows[:, tile(c)], ident[:, :])
                    mm.then_inc(rows_full, 1)
                def query_or_key(k, w):
                    for n in range(2):
                        free(uses, k + n)
                        for j in range(2):
                            at_w = slice(w + j * DK, w + (j + 1) * DK)
                            mm = split(bank(k + n), [v[:, at_w] for v in (qkv_hi, qkv_lo)],
                                       [v[:, j, half(n)] for v in (xc_hi, xc_lo)], j == 0, j == 1)
                        mm.then_inc(wide_full, 1)

                def values(m):
                    pe.wait_ge(xm_low, h * 2 + (m + 1))
                    for k in at["v"][2 * m:2 * m + 2]:
                        free(uses, k)
                        for i in range(2):
                            t = 2 * (at["v"].index(k) % 2) + i
                            for j in range(2):
                                w = 4 * DK + j * DV
                                mm = split(bank(k)[:, i * DV:(i + 1) * DV], [v[:, j, tile(t)] for v in (xm_hi, xm_lo)],
                                           [v[:, w:w + DV] for v in (qkv_hi, qkv_lo)], j == 0, j == 1)
                        mm.then_inc(wide_full, 1)

                pe.wait_ge(qkv_low, h + 1)
                pe.wait_ge(xc_low, h * 2 + 2)
                query_or_key(at["q"], 0)
                values(0)
                query_or_key(at["k"], 2 * DK)
                values(1)

                def scores(c):
                    pe.transpose(ps_s[:, P:2 * P], kT[:, tile(c)], ident[:, :])
                    pe.matmul(ps_s[:, 0:P], kT[:, tile(c)], qT[:, tile(c)], start=True, stop=True).then_inc(s_full, 1)

                def outputs(c):
                    if c == 0:
                        for n in range(4):
                            wait_taken(pe, uses, at["v"][n])
                    pe.wait_ge(s_taken, h * NC + (c + 1))
                    if not (first and c == 0):
                        pe.wait_ge(state_ready, h * NC + c)
                    pe.matmul(ps_intra[:, 0:DV + 1], sT[:, :], v_sb[:, c, :], start=True, stop=True)
                    pe.matmul(ps_inter[:, 0:DV + 1], qT[:, tile(c)], state[:, :], start=True, stop=True)
                    pe.matmul(ps_state[:, 0:DV + 1], kw[:, :], v_sb[:, c, :], start=True, stop=True).then_inc(num_full, 1)

                for n in range(2):
                    wait_taken(pe, uses, at["k"] + n)
                scores(0)
                chunk = [0]

                def core():
                    c = chunk[0]
                    outputs(c)
                    if c + 1 < NC:
                        scores(c + 1)
                    chunk[0] += 1

                for j in range(2):
                    in_slot(uses, s0, at["s_o"] + j, at["o"] + 2 * j, core)

            head(0, FIRST, True)
            with pe.Fori(1, HEADS) as h:
                head(h, LATER, False)
            def turn_x(n):
                m, t = n // KT, n % KT
                if t == 0:
                    pe.wait_ge(ln_x, 4 * m + 4)
                turn(BETWEEN, BRIDGE_X[n], [acc[:, 4 * m + i, tile(t)] for i in range(4)])

            ws = []
            for k, (kind, i) in enumerate(BRIDGE):
                if kind == "T":
                    turn_hn(HEADS - 1, BETWEEN, BRIDGE_T, (i,))
                elif kind == "O":
                    if i < 2:
                        ws.append(slot(SLOT_LAST_OUT, i))
                    if i % 2 == 0:
                        wait_y(4 * HEADS - 4, i // 2)
                    out_product(BETWEEN, k, ws[i % 2], i // 2)
                elif kind == "X":
                    turn_x(i)
                elif kind == "U":
                    if i == 0:
                        for part_lo in x1_lo:
                            pe.wait_ge(part_lo, KT // 2)
                    in_product(BETWEEN, k, 0, slot(SLOT_POOL, i))

            def group(g, first, last):
                uses, s0 = group_uses(g), g * SLOTS_PER_GROUP + SLOT_POOL
                y0 = g * 8 + 4 * HEADS
                if first:
                    for part_lo in x1_lo:
                        pe.wait_ge(part_lo, KT)
                    for j in range(2):
                        in_product(uses, 2 + j, 1, slot(s0, GS_U + j))
                for j in range(2 if first else 0, 4):
                    in_slot(uses, s0, GS_U + j, G_U + 2 * j)

                def z_and_mix(p):
                    for j in range(2):
                        in_slot(uses, s0, GS_Z[p] + j, G_Z[p] + 2 * j)
                    if p:
                        project(uses, G_OUT[0], s0, GS_OUT[0], y0)
                    else:
                        pe.wait_ge(pool_ready, g * 4 + 4)
                    w = slot(s0, GS_MIX[p])
                    for m in range(4):
                        n, j, k = m // 2, m % 2, G_MIX[p] + m
                        free(uses, k)
                        for t in range(4):
                            at = t * 2 * P + j * P
                            mm = split(bank(k), [v[:, at:at + P] for v in w],
                                       [v[:, t, half(n)] for v in (p_hi, p_lo)], t == 0, t == 3)
                        mm.then_inc(wide_full, 1)

                z_and_mix(0)
                z_and_mix(1)
                (project_by_token if last else project)(uses, G_OUT[1], s0, GS_OUT[1], y0 + 4)

            group(0, True, False)
            with pe.Fori(1, GROUPS - 1) as g:
                group(g, False, False)
            group(GROUPS - 1, False, True)


_INS = ("x", "mlstm_w_in", "mlstm_conv_w", "mlstm_conv_b", "mlstm_w_q", "mlstm_w_k", "mlstm_w_v", "mlstm_b_i",
        "mlstm_b_f", "mlstm_norm_g", "mlstm_skip", "mlstm_w_out", "pool_w_in", "pool_w_group", "pool_scale",
        "pool_w_out", "post_ln_g", "post_ln_b")
_KEEP_LAYER_AXIS = ("mlstm_conv_b", "mlstm_b_i", "mlstm_b_f", "mlstm_norm_g", "mlstm_skip", "pool_scale",
                    "post_ln_g", "post_ln_b")


def kernel(**inputs):
    from concourse import bacc
    from concourse.bass_utils import run_bass_kernel_spmd

    nc = bacc.Bacc("TRN2", target_bir_lowering=False, num_devices=1)
    arrays, args = {}, []
    for name in _INS:
        a = np.ascontiguousarray(inputs[name])
        if name not in _KEEP_LAYER_AXIS:
            a = a[0]
        arrays[f"in_{name}"] = a
        args.append(nc.dram_tensor(f"in_{name}", a.shape, F32, kind="ExternalInput").ap())
    out = nc.dram_tensor("out", (S, D), F32, kind="ExternalOutput").ap()
    build(nc, *args, out)
    got = run_bass_kernel_spmd(nc, [arrays], core_ids=[0])
    return got.results[0]["out"].reshape(1, S, D)
```

```python
from contextlib import ExitStack

import numpy as np

import concourse.bass as bass
import concourse.mybir as mybir
from concourse.alu_op_type import AluOpType as ALU

ACT = mybir.ActivationFunctionType
F32 = mybir.dt.float32
F32R = mybir.dt.float32r

P = 128
S = 1024
D = 1024
E = 2048
HEADS = 8
DV = E // HEADS
DK = DV // 2
CONV = 4
CHUNK = 128
NC = S // CHUNK
KT = D // P
ET = E // P
HALF = 512
SLOT = 1024
WINDOWS = (2, 4, 8, 16)
GROUPS = len(WINDOWS)
CG = E // GROUPS
PAD = 16
HALO = CONV - 1
EPS = 1e-5
ALPHA = 4.0 ** 0.25
FAR = 1e30

USE_X = [*range(8), *range(11, 19)]
USE_PAR = (9, 10)
USE_GATES = (8, 19)
USE_HEAD0 = 20
USES_PER_HEAD = 40
USE_LAST_OUT = USES_PER_HEAD * HEADS
TAIL_OUT = [*((t, n) for t in range(6) for n in range(2)), (6, 0), (7, 0), (6, 1), (7, 1)]
BRIDGE = [("T", 0), ("T", 1), *(("O", i) for i in range(4)), ("T", 2), ("T", 3), *(("O", i) for i in range(4, 12)),
          ("X", 0), ("X", 1), ("O", 12), ("X", 2), ("O", 13), ("X", 3), ("O", 14), ("X", 4), ("O", 15),
          ("X", 5), ("X", 6), ("X", 7), ("U", 0), ("U", 1)]
BRIDGE_WIDE = [step for step in BRIDGE if step[0] != "X"]
BRIDGE_T, BRIDGE_O, BRIDGE_U = ([k for k, (kind, _) in enumerate(BRIDGE_WIDE) if kind == which] for which in "TOU")
X_IN_U = [{7: (8, 9, 10)}, {1: (11,), 2: (12,), 4: (13,), 5: (14,), 7: (15,)}]
USE_POOL = USE_LAST_OUT + len(BRIDGE_WIDE) - 2
LAST_PROJECT = [(0, 0), (1, 0), (0, 1), (1, 1), *((t, n) for t in range(2, NC) for n in range(2))]
USES_PER_GROUP = 56
SLOTS_PER_HEAD = 8
SLOT_LAST_OUT = SLOTS_PER_HEAD * HEADS - 2
SLOT_POOL = SLOTS_PER_HEAD * HEADS
SLOTS_PER_GROUP = 14

FIRST = dict(xm=(0, 2), z=4, q=8, k=12, v=(10, 11, 14, 15), o=16, s_xm=0, s_z=2, s_o=4, slots=6)
LATER = dict(xm=(0, 6), hn=2, out=8, z=24, q=28, k=32, v=(30, 31, 34, 35), o=36, s_xm=0, s_out=2, s_z=4, s_o=6, slots=8)
G_U, G_Z, G_MIX, G_OUT = 0, (8, 16), (12, 36), (20, 40)
GS_U, GS_Z, GS_MIX, GS_OUT = 0, (4, 7), (6, 11), (9, 12)

COL_W, COL_B, COL_G, COL_SKIP = 0, 4 * ET, 5 * ET, 6 * ET
COL_SCALE, COL_LNG, COL_LNB = P, P + ET, P + ET + KT
COLS = COL_LNB + KT

ACT_LN, ACT_EI, ACT_ROWS = 5, 7 + NC, 7 + 2 * NC
VEC_M, VEC_PREV, VEC_ROWS = 5, 7, 8
VEC_START, VEC_FIRST, VEC_LATER = 4, 68, 58
VEC_BETWEEN, VEC_GROUP = 2, 20
SET_IDENT, SET_PAR, CONST_SETS = 2, 4, 14
POOL_SETS = 4 + 3 * GROUPS + sum(win - 1 for win in WINDOWS)
LATE = NC - 2


def formed(n):
    return (1, n - n // 4) if n % 4 else (0, n // 4 + 1)


class Uses:

    def __init__(self, base, quarter):
        self.base, self.quarter = base, quarter

    def full(self, k):
        return self.base + (k + 1)

    def taken(self, k):
        return self.quarter + (k // 4 + 1)


START = Uses(0, 0)
BETWEEN = Uses(USE_LAST_OUT, USE_LAST_OUT // 4)


def head_uses(h):
    if isinstance(h, int) and h == 0:
        return Uses(USE_HEAD0, USE_HEAD0 // 4)
    return Uses(h * USES_PER_HEAD, h * (USES_PER_HEAD // 4))


def group_uses(g):
    return Uses(g * USES_PER_GROUP + USE_POOL, g * (USES_PER_GROUP // 4) + USE_POOL // 4)


def build(nc, x, w_in, conv_w, conv_b, w_q, w_k, w_v, b_i, b_f, norm_g, skip, w_out,
          p_in, p_group, p_scale, p_out, ln_g, ln_b, out):
    m_rows = nc.dram_tensor("m_rows", (HEADS, S), F32, kind="Internal").ap()
    wc_rows = nc.dram_tensor("wc_rows", (HEADS, NC), F32, kind="Internal").ap()
    with ExitStack() as ctx:
        def sb(name, shape, dt=F32, where=ctx):
            return where.enter_context(nc.sbuf_tensor(name, shape, dt))

        def pb(name, shape):
            return ctx.enter_context(nc.psum_tensor(name, shape, F32))

        def sem(name):
            return ctx.enter_context(nc.semaphore(name))

        with ExitStack() as behind:
            normed_out = sb("normed_out", [P, NC, D], where=behind)
        x_hi = sb("x_hi", [P, KT, S], F32R)
        x_lo = sb("x_lo", [P, KT, S], F32R)
        acc = sb("acc", [P, NC, D])
        w_raw = sb("w_raw", [P, 2, SLOT])
        w_hi = sb("w_hi", [P, 2, SLOT], F32R)
        w_lo = sb("w_lo", [P, 2, SLOT], F32R)
        gate_t = sb("gate_t", [P, 2, HALF])
        ident = sb("ident", [P, P])
        cols = sb("cols", [P, COLS])
        stats = sb("stats", [P, NC, 6])
        mv = sb("mv", [P, NC, 2])
        nhalf = sb("nhalf", [P, NC])
        rstd = sb("rstd", [P, NC])
        small = sb("small", [P, 4, NC])

        with ExitStack() as gates:
            e_buf = sb("e_buf", [P, 2, S], where=gates)
            f_buf = sb("f_buf", [P, 2, S], where=gates)
        y_hi = sb("y_hi", [P, 2, S], F32R)
        y_lo = sb("y_lo", [P, 2, S], F32R)

        with ExitStack() as own:
            def sa(name, shape, dt=F32):
                return sb(name, shape, dt, own)
            xm = sa("xm", [P, 2, HALO + S])
            with ExitStack() as whole:
                xc = sb("xc", [P, 2, S], where=whole)
            xc_lo = sa("xc_lo", [P, 2, S], F32R)
            with ExitStack() as conv:
                tmp_a = sb("tmp_a", [P, S], where=conv)
                tmp_c = sb("tmp_c", [P, S], where=conv)
            xm_hi = sa("xm_hi", [P, 2, HALF], F32R)
            xm_lo = sa("xm_lo", [P, 2, HALF], F32R)
            with ExitStack() as whole:
                w_qkv = sb("w_qkv", [P, SLOT], where=whole)
            qkv_lo = sa("qkv_lo", [P, SLOT], F32R)
            qkv_hi = sa("qkv_hi", [P, SLOT], F32R)
            qT = sa("qT", [P, S])
            kT = sa("kT", [P, S])
            m_bc = sa("m_bc", [P, S])
            v_sb = sa("v_sb", [P, NC, DV + 1])
            with ExitStack() as early:
                xc_hi = sb("xc_hi", [P, 2, S], F32R, early)
            num = sa("num", [P, NC, DV + 1])
            g_packed = sa("g_packed", [P, KT, 2 * HEADS])
            mask = sa("mask", [P, P])
            dist = sa("dist", [P, P])
            wgt = sa("wgt", [P, P])
            sT = sa("sT", [P, P])
            kw = sa("kw", [P, P])
            state = sa("state", [P, DV + 1])
            gcol = sa("gcol", [P, NC, 4, HEADS])
            wc_bc = sa("wc_bc", [P, HEADS * NC])
            bias = sa("bias", [P, 1])

        with ExitStack() as own:
            def sB(name, shape, dt=F32):
                return sb(name, shape, dt, own)
            with ExitStack() as ahead:
                x_new = sb("x_new", [P, 4, HALF], where=ahead)
            with ExitStack() as behind:
                g_bc = sb("g_bc", [P, D], where=behind)
                b_bc = sb("b_bc", [P, D], where=behind)
            p_hi = sB("p_hi", [P, 4, S], F32R)
            p_lo = sB("p_lo", [P, 4, S], F32R)
            u_buf = sB("u_buf", [P, 2, PAD + S])
            win_a = sB("win_a", [P, PAD + S])
            win_b = sB("win_b", [P, PAD + S])
            zz = sB("zz", [P, 2, S])
            y_t = sB("y_t", [P, 2, HALF])
            flag = sB("flag", [P, GROUPS * GROUPS])
            inv_win = sB("inv_win", [P, GROUPS])
            head_fix = sB("head_fix", [P, GROUPS * PAD])
            b_first = sB("b_first", [P, D])

        g_first = y_t[:, :, :].rearrange("p a b -> p (a b)")
        normed = [normed_out[:, t, :] for t in range(NC)]
        squares_a, squares_b = tmp_a[:, :], x_lo[:, 0, :]

        wide = pb("wide", [P, 4, HALF])
        ps_s = pb("ps_s", [P, HALF])
        ps_intra = pb("ps_intra", [P, HALF])
        ps_inter = pb("ps_inter", [P, HALF])
        ps_state = pb("ps_state", [P, HALF])
        x_banks = (ps_s, ps_intra, ps_inter, ps_state)

        par_rows = tmp_c[:, 0:2 * P].rearrange("p (b n) -> p b n", b=2)
        g_raw = tmp_a[:, :]
        g_hi, g_lo = y_hi[:, 0, :], y_lo[:, 0, :]
        HI, LF = slice(0, HEADS), slice(32, 32 + HEADS)
        rows = qT
        i_row, f_row = kT[HI, :], kT[LF, :]
        f_abs = tmp_c[LF, :]
        lf_row = tmp_c[HI, :]
        flat = num[:, :, :].rearrange("p c d -> p (c d)")
        bcum, m_row = flat[HI, 0:S], flat[HI, S:2 * S]
        carry, keep = xc[HI, 0, :], xc[HI, 1, :]
        m_prev, m_last = small[HI, 0, :], small[HI, 1, :]
        w_chunk = small[LF, 2, :]

        def by_chunk(row):
            return row.rearrange("p (c t) -> p c t", t=CHUNK)

        x_in = [sem(f"x_in{t}") for t in range(NC)]
        const_set = sem("const_set")
        par_in = sem("par_in")
        rows_full = sem("rows_full")
        gw_in = sem("gw_in")
        gw_placed = sem("gw_placed")
        bias_in = sem("bias_in")
        gw_hi = sem("gw_hi")
        gw_lo = sem("gw_lo")
        raw_in = [sem("raw_in0"), sem("raw_in1")]
        hi_ready = sem("hi_ready")
        lo_ready = sem("lo_ready")
        wide_full = sem("wide_full")
        wide_taken = [sem(f"wide_taken{b}") for b in range(4)]
        xt_hi = sem("xt_hi")
        gate_act = sem("gate_act")
        gate_vec = sem("gate_vec")
        rows_out = sem("rows_out")
        m_in = sem("m_in")
        wc_in = sem("wc_in")
        qkv_in = sem("qkv_in")
        vec_step = sem("vec_step")
        conv_ready = sem("conv_ready")
        conv_tanh = sem("conv_tanh")
        z_tanh = sem("z_tanh")
        o_used = sem("o_used")
        xc_ready = sem("xc_ready")
        xc_high = sem("xc_high")
        xc_low = sem("xc_low")
        qkv_high = sem("qkv_high")
        qkv_low = sem("qkv_low")
        xm_high = sem("xm_high")
        xm_low = sem("xm_low")
        y_sum = sem("y_sum")
        y_rounded = sem("y_rounded")
        y_ready = sem("y_ready")
        dist_ready = sem("dist_ready")
        wgt_ready = sem("wgt_ready")
        s_full = sem("s_full")
        s_taken = sem("s_taken")
        num_full = sem("num_full")
        intra_taken = sem("intra_taken")
        state_ready = sem("state_ready")
        var_ready = sem("var_ready")
        rstd_ready = sem("rstd_ready")
        hn_ready = sem("hn_ready")
        ln_mean = sem("ln_mean")
        ln_squares = sem("ln_squares")
        ln_var = sem("ln_var")
        ln_rstd = sem("ln_rstd")
        ln_x = sem("ln_x")
        x1_full = sem("x1_full")
        x1_taken = [sem("x1_taken0"), sem("x1_taken1")]
        x1_hi = sem("x1_hi")
        x1_lo = [sem("x1_lo0"), sem("x1_lo1")]
        gb_in = sem("gb_in")
        acc_gain = sem("acc_gain")
        acc_ready = sem("acc_ready")
        pool_set = sem("pool_set")
        pool_sum = sem("pool_sum")
        pool_rounded = sem("pool_rounded")
        pool_ready = sem("pool_ready")
        ln_gain = sem("ln_gain")
        ln_scaled = sem("ln_scaled")
        ln_done = sem("ln_done")
        ln_done_late = sem("ln_done_late")
        stored = sem("stored")

        block = ctx.enter_context(nc.Block())

        def link(eng, ins, s, value):
            ins.then_inc(s, 1)
            eng.wait_ge(s, value)

        def link_taken(eng, ins, uses, k):
            link(eng, ins, wide_taken[k % 4], uses.taken(k))

        def wait_taken(eng, uses, k):
            eng.wait_ge(wide_taken[k % 4], uses.taken(k))

        def bank(k):
            return wide[:, k % 4, :]

        def half(n):
            return slice(n * HALF, (n + 1) * HALF)

        def tile(t):
            return slice(t * P, (t + 1) * P)

        def x_part(v, n):
            return v[:, 4 * (n % 2):4 * (n % 2) + 4, tile(n // 2)]

        def by_feature_tile(k):
            return bank(k).rearrange("p (f t) -> p f t", f=4)

        def x_bank(n):
            return x_banks[n % 4][:, :]

        def col(i):
            return cols[:, bass.ds(i, 1)]

        def slot_base(h):
            return 0 if isinstance(h, int) and h == 0 else h * SLOTS_PER_HEAD - 2

        @block.sync
        def _(sp):
            def load_x(ts):
                for t in ts:
                    sp.dma_start(acc[:, t, :], x[t * P:(t + 1) * P, :]).then_inc(x_in[t], 16)

            load_x(range(4))
            sp.wait_ge(const_set, SET_PAR)
            sp.dma_start(par_rows[0:COL_B, 0, :], conv_w.rearrange("k (t p) -> (k t) p", p=P)).then_inc(par_in, 16)
            for c, v in ((COL_B, conv_b), (COL_G, norm_g), (COL_SKIP, skip)):
                sp.dma_start(par_rows[c:c + ET, 0, :], v.rearrange("o (t p) -> (o t) p", p=P)).then_inc(par_in, 16)
            for c, v in ((COL_SCALE, p_scale), (COL_LNG, ln_g[0:1, :]), (COL_LNB, ln_b[0:1, :])):
                sp.dma_start(par_rows[c - P:c - P + v.shape[1] // P, 1, :],
                             v.rearrange("o (t p) -> (o t) p", p=P)).then_inc(par_in, 16)

            def load_slot(s, k, src):
                if k is None:
                    k = s
                else:
                    sp.wait_ge(lo_ready, s - 1)
                dst = w_raw[:, k % 2, :].rearrange("p (k n) -> p k n", k=src.shape[1])
                sp.dma_start(dst, src).then_inc(raw_in[k % 2], 16)

            def in_cols(w, c):
                return w[:, bass.ds(c, P)].rearrange("(k p) n -> p k n", p=P)

            def out_rows(w, r, n):
                return w[bass.ds(r, 2 * P), half(n)].rearrange("(k p) n -> p k n", p=P)

            def load_qkv(h):
                for i, (w, n) in enumerate(((w_q, DK), (w_k, DK), (w_v, DV))):
                    sp.dma_start(w_qkv[:, i * 2 * DK:i * 2 * DK + 2 * n].rearrange("p (k n) -> p k n", k=2),
                                 w[bass.ds(h, 1), :, :].rearrange("o (k p) n -> p (o k) n", p=P)).then_inc(qkv_in, 16)

            load_x(range(4, NC))
            load_slot(0, None, in_cols(w_in, 0))
            load_slot(1, None, in_cols(w_in, P))
            load_qkv(0)
            for j in range(2):
                load_slot(2 + j, j, in_cols(w_in, E + j * P))
            sp.wait_ge(gate_vec, VEC_M)
            sp.dma_start(m_rows, m_row).then_inc(rows_out, 16)
            sp.wait_ge(gate_act, ACT_EI)
            sp.dma_start(wc_rows, w_chunk).then_inc(rows_out, 16)
            sp.wait_ge(rows_out, 32)
            sp.dma_start(wc_bc[:, :], wc_rows.rearrange("h c -> (h c)").partition_broadcast(P)).then_inc(wc_in, 16)
            sp.dma_start(m_bc[:, :], m_rows[0, :].partition_broadcast(P)).then_inc(m_in, 16)
            for j in range(2):
                load_slot(4 + j, j, in_cols(w_in, 2 * E + j * P))

            with sp.Fori(1, HEADS) as h:
                s0 = slot_base(h)
                for j in range(2):
                    load_slot(s0 + j, j, in_cols(w_in, h * DV + j * P))
                sp.wait_ge(wide_full, head_uses(h).full(LATER["v"][3] - USES_PER_HEAD))
                load_qkv(h)
                for n in range(2):
                    load_slot(s0 + 2 + n, n, out_rows(w_out, h * DV - DV, n))
                for j in range(2):
                    load_slot(s0 + 4 + j, j, in_cols(w_in, h * DV + (E + j * P)))
                sp.wait_ge(dist_ready, h * NC)
                sp.dma_start(m_bc[:, :], m_rows[bass.ds(h, 1), :].rearrange("o t -> (o t)")
                             .partition_broadcast(P)).then_inc(m_in, 16)
                for j in range(2):
                    load_slot(s0 + 6 + j, j, in_cols(w_in, h * DV + (2 * E + j * P)))

            for n in range(2):
                load_slot(SLOT_LAST_OUT + n, n, out_rows(w_out, (HEADS - 1) * DV, n))
            sp.wait_ge(wide_full, BETWEEN.full(BRIDGE_T[-1]))
            sp.dma_start(g_first, ln_g[0, :].partition_broadcast(P)).then_inc(gb_in, 16)
            sp.dma_start(b_first[:, :], ln_b[0, :].partition_broadcast(P)).then_inc(gb_in, 16)

            def group_loads(g, last):
                s0 = g * SLOTS_PER_GROUP + SLOT_POOL
                for j in range(4):
                    load_slot(s0 + j, j, in_cols(p_in, g * CG + j * P))
                for p in range(2):
                    for j in range(2):
                        load_slot(s0 + GS_Z[p] + j, GS_Z[p] + j, in_cols(p_in, g * CG + (E + (2 * p + j) * P)))
                    if p == 1:
                        for n in range(2):
                            load_slot(s0 + GS_OUT[0] + n, GS_OUT[0] + n, out_rows(p_out, g * CG, n))
                        load_mix(g, s0, 1)
                        for n in range(2):
                            load_slot(s0 + GS_OUT[1] + n, GS_OUT[1] + n, out_rows(p_out, g * CG + 2 * P, n))
                    else:
                        load_mix(g, s0, 0)

            def load_mix(g, s0, p):
                load_slot(s0 + GS_MIX[p], GS_MIX[p], p_group[bass.ds(g, 1), :, p * 2 * P:(p + 1) * 2 * P]
                          .rearrange("o (k p) n -> p (o k) n", p=P))

            with sp.Fori(0, GROUPS - 1) as g:
                group_loads(g, False)
            group_loads(GROUPS - 1, True)
            sp.wait_ge(wide_full, group_uses(GROUPS - 1).full(G_MIX[1] + 3))
            sp.dma_start(g_bc[:, :], ln_g[1, :].partition_broadcast(P)).then_inc(gb_in, 16)
            sp.dma_start(b_bc[:, :], ln_b[1, :].partition_broadcast(P)).then_inc(gb_in, 16)
            for t in range(NC):
                if t < LATE:
                    sp.wait_ge(ln_done, t + 1)
                    sp.dma_start(out[t * P:(t + 1) * P, :], normed[t]).then_inc(stored, 16)
                    continue
                for n in range(2):
                    sp.wait_ge(ln_done_late, 2 * (t - LATE) + n + 1)
                    sp.dma_start(out[t * P:(t + 1) * P, half(n)], normed[t][:, half(n)]).then_inc(stored, 16)
            sp.wait_ge(stored, 16 * (LATE + 2 * (NC - LATE)))

        @block.gpsimd
        def _(pool):
            sets = [
                lambda: pool.memset(ident[:, :], 0.0),
                lambda: pool.affine_select(out=ident[:, :], in_=ident[:, :], compare_op=ALU.not_equal, fill=1.0,
                                           base=0, pattern=[[-1, P]], channel_multiplier=1),
                lambda: pool.memset(g_raw, 0.0),
                lambda: pool.memset(par_rows, 0.0),
                lambda: pool.memset(mask[:, :], 0.0),
                lambda: pool.affine_select(out=mask[:, :], in_=mask[:, :], compare_op=ALU.is_ge, fill=FAR,
                                           base=0, pattern=[[1, P]], channel_multiplier=-1),
                lambda: pool.memset(rows[:, :], 0.0),
                lambda: pool.memset(keep, 1.0),
                lambda: pool.memset(by_chunk(keep)[:, :, 0:1], 0.0),
                lambda: pool.memset(carry, 0.0),
                lambda: pool.memset(small[:, :, :], 0.0),
                lambda: pool.memset(v_sb[:, :, DV:DV + 1], 1.0),
                lambda: pool.memset(xm[:, :, 0:HALO], 0.0),
                lambda: pool.memset(nhalf[:, :], -0.5),
            ]
            assert len(sets) == CONST_SETS
            for n, f in enumerate(sets):
                link(pool, f(), const_set, n + 1)

            pool.wait_ge(gw_in, 16)
            for n, at in enumerate((HI, LF)):
                link(pool, pool.tensor_copy(g_raw.rearrange("p (k n) -> p k n", k=KT)[:, :, at],
                                            g_packed[:, :, n * HEADS:(n + 1) * HEADS]), gw_placed, n + 1)

            def make_lo(s, k):
                pool.wait_ge(hi_ready, s + 1)
                link(pool, pool.tensor_tensor(w_lo[:, k % 2, :], w_raw[:, k % 2, :],
                                              w_hi[:, k % 2, :].bitcast(F32), ALU.subtract), lo_ready, s + 1)

            def power(ready, done, n, dst, src, k):
                pool.wait_ge(ready, n)
                link(pool, pool.tensor_tensor(dst, src, nhalf[:, 0:k], ALU.pow), done, n)

            def head(h, at):
                s0 = slot_base(h)
                for k in range(2, at["slots"]):
                    make_lo(s0 + k, k)
                    if k == 3:
                        pool.wait_ge(qkv_high, h + 1)
                        link(pool, pool.tensor_tensor(qkv_lo[:, :], w_qkv[:, :], qkv_hi[:, :].bitcast(F32),
                                                      ALU.subtract), qkv_low, h + 1)

                def powers(f):
                    part = slice(4 * f, 4 * f + 4)
                    power(var_ready, rstd_ready, h * 2 + (f + 1), rstd[:, part], small[:, 3, part], 4)

                powers(0)
                for f in range(2):
                    make_lo(s0 + (at["slots"] + f), f)
                powers(1)

            def deviation(t, n):
                pool.wait_ge(ln_squares, n + t + 1)
                link(pool, pool.tensor_scalar(small[:, 3, t:t + 1], small[:, 3, t:t + 1], 1.0 / D, EPS,
                                              ALU.mult, ALU.add), ln_var, n + t + 1)
                link(pool, pool.tensor_tensor(rstd[:, t:t + 1], small[:, 3, t:t + 1], nhalf[:, 0:1], ALU.pow),
                     ln_rstd, n + t + 1)

            make_lo(0, 0)
            make_lo(1, 1)
            head(0, FIRST)
            with pool.Fori(1, HEADS) as h:
                head(h, LATER)
            sets = [lambda part=part: pool.memset(part, 0.0)
                    for part in (u_buf[:, :, 0:PAD], win_a[:, 0:PAD], win_b[:, 0:PAD], flag[:, :])]
            for g, win in enumerate(WINDOWS):
                at = g * PAD
                for part, value in ((flag[:, g * GROUPS:g * GROUPS + g + 1], 1.0), (inv_win[:, g:g + 1], 1.0 / win),
                                    (head_fix[:, at:at + PAD], 1.0),
                                    *((head_fix[:, at + t:at + t + 1], win / (t + 1)) for t in range(win - 1))):
                    sets.append(lambda part=part, value=value: pool.memset(part, value))
            assert len(sets) == POOL_SETS

            def low_even(ns):
                for n in ns:
                    pool.wait_ge(x1_hi, n + 1)
                    dst = (slice(None), n % KT, half(n // KT))
                    link(pool, pool.tensor_tensor(x_lo[dst], x_new[:, n % 4, :], x_hi[dst].bitcast(F32),
                                                  ALU.subtract), x1_lo[0], n // 2 + 1)

            n = 0
            for t in range(6):
                deviation(t, 0)
                if t == 1:
                    pool.wait_ge(wide_full, BETWEEN.full(BRIDGE_T[-1]))
                if t >= 1:
                    for f in sets[(t - 1) * 9:t * 9]:
                        n += 1
                        link(pool, f(), pool_set, n)
            assert n == POOL_SETS
            low_even((0, 2))
            make_lo(SLOT_POOL, 0)
            low_even((4, 6))
            for t in (6, 7):
                deviation(t, 0)
            make_lo(SLOT_POOL + 1, 1)
            low_even(range(8, 16, 2))
            shifts = {3: (0,), 4: (1,), 6: (2, 3), 7: (4, 5), 8: (6, 7)}
            for k in range(2, SLOTS_PER_GROUP + 2):
                make_lo(SLOT_POOL + k, k)
                for t in shifts.get(k, ()):
                    pool.wait_ge(acc_gain, t + 1)
                    link(pool, pool.tensor_tensor(acc[:, t, :], acc[:, t, :], b_first[:, :], ALU.add),
                         acc_ready, t + 1)
            with pool.Fori(1, GROUPS - 1) as g:
                s0 = g * SLOTS_PER_GROUP + SLOT_POOL
                for k in range(2, SLOTS_PER_GROUP + 2):
                    make_lo(s0 + k, k)
            s0 = (GROUPS - 1) * SLOTS_PER_GROUP + SLOT_POOL
            for k in range(2, SLOTS_PER_GROUP):
                make_lo(s0 + k, k)
            pool.wait_ge(gb_in, 64)
            for t in range(NC):
                deviation(t, NC)
                if 0 < t <= LATE:
                    pool.wait_ge(ln_scaled, t)
                    link(pool, pool.tensor_tensor(normed[t - 1], normed[t - 1], b_bc[:, :], ALU.add),
                         ln_done, t)

        @block.scalar
        def _(act):
            def make_hi(s, k):
                act.wait_ge(raw_in[k % 2], (s - k % 2) * 8 + 16)
                link(act, act.activation(w_hi[:, k % 2, :], w_raw[:, k % 2, :], ACT.Copy), hi_ready, s + 1)

            def take(uses, k, dst, scale=1.0):
                act.wait_ge(wide_full, uses.full(k))
                link_taken(act, act.activation(dst, bank(k), ACT.Copy, scale=scale), uses, k)

            def round_x(ns):
                for n in ns:
                    k = USE_X[n]
                    act.wait_ge(wide_full, k + 1)
                    link(act, act.activation(x_part(x_hi, n), by_feature_tile(k), ACT.Copy), xt_hi, n + 1)

            n = [0]

            def gate(ins):
                n[0] += 1
                link(act, ins, gate_act, n[0])

            def gate_rows(m):
                k = USE_GATES[m]
                act.wait_ge(wide_full, k + 1)
                gate(act.activation(i_row[:, half(m)], wide[HI, k % 4, :], ACT.Identity, bias=bias[HI, :]))
                link_taken(act, act.activation(f_row[:, half(m)], wide[LF, k % 4, :], ACT.Identity,
                                               bias=bias[LF, :]), START, k)

            act.dma_start(g_packed[:, :, :], w_in[:, 3 * E:3 * E + 2 * HEADS].rearrange("(k p) n -> p k n", p=P)
                          ).then_inc(gw_in, 16)
            act.dma_start(bias[HI, :], b_i.rearrange("o h -> h o")).then_inc(bias_in, 16)
            act.dma_start(bias[LF, :], b_f.rearrange("o h -> h o")).then_inc(bias_in, 16)
            round_x(range(4))
            act.wait_ge(gw_placed, 2)
            link(act, act.activation(g_hi, g_raw, ACT.Copy), gw_hi, 1)
            round_x(range(4, KT))
            act.wait_ge(bias_in, 32)
            gate_rows(0)
            round_x(range(KT, 2 * KT))
            make_hi(0, 0)
            make_hi(1, 1)
            gate_rows(1)
            gate(act.activation(f_abs, f_row, ACT.Abs))
            gate(act.activation(f_abs, f_abs, ACT.Exp, scale=-1.0))
            gate(act.activation(f_abs, f_abs, ACT.Ln, bias=1.0))
            assert n[0] == ACT_LN

            def gate_em():
                act.preload_act_table(ACT.Tanh)
                act.wait_ge(gate_vec, VEC_ROWS)
                gate(act.activation(rows[64:64 + HEADS, :], lf_row, ACT.Exp, scale=-1.0))

            def gate_ei_ws():
                for c in range(NC):
                    gate(act.activation(rows[LF, tile(c)], m_row[:, tile(c)], ACT.Exp, scale=-1.0,
                                        bias=m_prev[:, c:c + 1]))
                gate(act.activation(w_chunk, by_chunk(rows[LF, :])[:, :, CHUNK - 1], ACT.Copy))
                assert n[0] == ACT_EI
                for c in range(NC):
                    gate(act.activation(rows[96:96 + HEADS, tile(c)], rows[HI, tile(c)], ACT.Exp,
                                        bias=m_last[:, c:c + 1]))
                assert n[0] == ACT_ROWS

            def round_y(n, m, src):
                link(act, act.activation(y_hi[:, m % 2, half(m // 2)], src, ACT.Copy), y_rounded, n)

            def prev_y(h, ms):
                for m in ms:
                    act.wait_ge(y_sum, h * 4 + (m + 1))
                    round_y(h * 4 + (m + 1), m, tmp_c[:, half(m % 2)])

            def head(h, at, first):
                uses, s0 = head_uses(h), slot_base(h)

                def conv_gate(j):
                    act.wait_ge(conv_ready, h * 2 + (j + 1))
                    link(act, act.activation(tmp_c[:, :], tmp_a[:, :], ACT.Tanh), conv_tanh, h * 2 + (j + 1))

                for j in range(2):
                    for n in range(2):
                        k = at["xm"][j] + n
                        take(uses, k, xm[:, j, HALO + n * HALF:HALO + (n + 1) * HALF])
                        if j == 0 and n == 1:
                            make_hi(s0 + 2, 0)
                            if not first:
                                prev_y(h - 1, range(3))
                        if j == 1 and n == 0:
                            if first:
                                gate_em()
                                conv_gate(0)
                            else:
                                prev_y(h - 1, range(3, 4))
                make_hi(s0 + 3, 1)
                act.wait_ge(qkv_in, h * 48 + 48)
                link(act, act.activation(qkv_hi[:, :], w_qkv[:, :], ACT.Copy), qkv_high, h + 1)

                def round_xc(j):
                    act.wait_ge(xc_ready, h * 2 + (j + 1))
                    link(act, act.activation(xc_hi[:, j, :], xc[:, j, :], ACT.Copy), xc_high, h * 2 + (j + 1))

                def round_xm(n):
                    link(act, act.activation(xm_hi[:, :, :], xm[:, :, HALO + n * HALF:HALO + (n + 1) * HALF],
                                             ACT.Copy), xm_high, h * 2 + (n + 1))

                def take_v(n):
                    k = at["v"][n]
                    act.wait_ge(wide_full, uses.full(k))
                    link_taken(act, act.activation(v_sb[:, 2 * n:2 * n + 2, 0:DV],
                                                   bank(k).rearrange("p (t d) -> p t d", t=2), ACT.Copy), uses, k)

                if first:
                    gate_ei_ws()
                    act.wait_ge(rows_out, 32)
                else:
                    conv_gate(0)
                    for n in range(2):
                        act.wait_ge(wide_full, uses.full(at["out"] + NC * (n + 1) - 1))
                        make_hi(s0 + (4 + n), n)
                conv_gate(1)
                for m in range(4):
                    k = at["z"] + m
                    act.wait_ge(wide_full, uses.full(k))
                    if m >= 2:
                        wait_taken(act, uses, k - 2)
                    link(act, act.activation(gate_t[:, m % 2, :], bank(k), ACT.Tanh, scale=0.5),
                         z_tanh, h * 4 + (m + 1))
                    if m % 2:
                        make_hi(s0 + (at["s_o"] + m // 2), m // 2)
                    if m < 2:
                        round_xc(m)
                    elif m == 2:
                        round_xm(0)
                for n in range(2):
                    take(uses, at["q"] + n, qT[:, half(n)], DK ** -0.5)
                take_v(0)
                act.wait_ge(wide_full, uses.full(at["v"][1]))
                round_xm(1)
                take_v(1)
                for n in range(2):
                    take(uses, at["k"] + n, kT[:, half(n)])
                for n in range(2, 4):
                    take_v(n)

                def decay(c):
                    act.wait_ge(dist_ready, h * NC + (c + 1))
                    link(act, act.activation(wgt[:, :], dist[:, :], ACT.Exp, scale=-1.0),
                         wgt_ready, h * NC + (c + 1))

                decay(0)
                for c in range(NC):
                    if c + 1 < NC:
                        decay(c + 1)
                    act.wait_ge(num_full, h * NC + (c + 1))
                    link(act, act.activation(num[:, c, :], ps_intra[:, 0:DV + 1], ACT.Copy),
                         intra_taken, h * NC + (c + 1))
                    if c % 2:
                        m = c // 2
                        k = at["o"] + m
                        act.wait_ge(wide_full, uses.full(k))
                        if m >= 2:
                            act.wait_ge(o_used, h * 4 + (m - 1))
                        link_taken(act, act.activation(gate_t[:, m % 2, :], bank(k), ACT.Tanh, scale=0.5), uses, k)
                        if m % 2:
                            make_hi(s0 + (at["slots"] + m // 2), m // 2)

            head(0, FIRST, True)
            with act.Fori(1, HEADS) as h:
                head(h, LATER, False)
            prev_y(HEADS - 1, range(2))

            def sum_squares(t, n, squares):
                act.wait_ge(ln_mean, n + t + 1)
                link(act, act.activation(squares, acc[:, t, :], ACT.Square, bias=small[:, 2, t:t + 1],
                                         accum_out=small[:, 3, t:t + 1]), ln_squares, n + t + 1)

            def form_x(n):
                t = n % KT
                if n >= 4:
                    act.wait_ge(x1_lo[0], (n - 4) // 2 + 1)
                act.wait_ge(x1_full, n + 1)
                link(act, act.activation(x_new[:, n % 4, :], x_bank(n), ACT.Identity,
                                         scale=cols[:, COL_LNG + t:COL_LNG + t + 1],
                                         bias=cols[:, COL_LNB + t:COL_LNB + t + 1]), x1_taken[0], formed(n)[1])

            def next_input(ns):
                for n in ns:
                    by, count = formed(n)
                    if by:
                        act.wait_ge(x1_taken[1], count)
                    else:
                        form_x(n)
                    link(act, act.activation(x_hi[:, n % KT, half(n // KT)], x_new[:, n % 4, :], ACT.Copy),
                         x1_hi, n + 1)

            for t in range(6):
                sum_squares(t, 0, squares_a)
                if t == 1:
                    prev_y(HEADS - 1, range(2, 4))
            next_input(range(4))
            act.wait_ge(wide_full, BETWEEN.full(BRIDGE_O[13]))
            make_hi(SLOT_POOL, 0)
            next_input(range(4, 8))
            for t in (6, 7):
                sum_squares(t, 0, squares_a)
            act.wait_ge(wide_full, BETWEEN.full(BRIDGE_O[15]))
            make_hi(SLOT_POOL + 1, 1)
            next_input(range(8, 10))
            act.wait_ge(pool_set, POOL_SETS)

            def group(g, first, last):
                uses, s0 = group_uses(g), g * SLOTS_PER_GROUP + SLOT_POOL

                def next_hi(k):
                    if k + 2 < SLOTS_PER_GROUP or not last:
                        make_hi(s0 + (k + 2), k)

                def round_pooled(j):
                    act.wait_ge(pool_sum, g * 4 + (j + 1))
                    link(act, act.activation(p_hi[:, j, :], win_a[:, PAD:PAD + S], ACT.Copy),
                         pool_rounded, g * 4 + (j + 1))

                def take_u(j, n):
                    take(uses, G_U + 2 * j + n, u_buf[:, j % 2, PAD + n * HALF:PAD + (n + 1) * HALF])

                def z_gate(p):
                    for m in range(4):
                        k = G_Z[p] + m
                        act.wait_ge(wide_full, uses.full(k))
                        if m >= 2:
                            wait_taken(act, uses, k - 2)
                        link(act, act.activation(gate_t[:, m % 2, :], bank(k), ACT.Tanh, scale=0.5),
                             z_tanh, g * 8 + (4 * HEADS + 4 * p + m + 1))
                        if p == 0 and m == 0:
                            round_pooled(3)
                        if m % 2:
                            next_hi(GS_Z[p] + m // 2)

                def mixed(p):
                    for m in range(4):
                        if m == 3:
                            act.wait_ge(wide_full, uses.full(G_MIX[p] + m))
                            next_hi(GS_MIX[p])
                        wait_taken(act, uses, G_MIX[p] + m)
                        round_y(g * 8 + (4 * HEADS + 4 * p + m + 1), m, y_t[:, m % 2, :])

                def projected(p):
                    for n in range(2):
                        act.wait_ge(wide_full, uses.full(G_OUT[p] + NC * (n + 1) - 1))
                        next_hi(GS_OUT[p] + n)

                if first:
                    take(BETWEEN, BRIDGE_U[0], u_buf[:, 0, PAD:PAD + HALF])
                    next_input(range(10, 15))
                    take(BETWEEN, BRIDGE_U[1], u_buf[:, 1, PAD:PAD + HALF])
                    next_input(range(15, 16))
                    for part_lo in x1_lo:
                        act.wait_ge(part_lo, KT)
                    for j in range(2):
                        take(uses, 2 + j, u_buf[:, j, PAD + HALF:PAD + S])
                        next_hi(GS_U + j)
                    round_pooled(0)
                for j in range(2 if first else 0, 4):
                    take_u(j, 0)
                    if j:
                        round_pooled(j - 1)
                    take_u(j, 1)
                    next_hi(GS_U + j)
                z_gate(0)
                mixed(0)
                z_gate(1)
                projected(0)
                mixed(1)
                if not last:
                    projected(1)

            group(0, True, False)
            with act.Fori(1, GROUPS - 1) as g:
                group(g, False, False)
            group(GROUPS - 1, False, True)
            for t in range(NC + 1):
                if t < NC:
                    sum_squares(t, NC, squares_b)
                if 0 < t <= LATE:
                    act.wait_ge(ln_gain, t)
                    act.wait_ge(ln_rstd, NC + t)
                    link(act, act.activation(normed[t - 1], normed[t - 1], ACT.Copy, scale=rstd[:, t - 1:t]),
                         ln_scaled, t)

        @block.vector
        def _(dve):
            base, steps = [0], [0]

            def step(ins, wait=True):
                steps[0] += 1
                ins.then_inc(vec_step, 1)
                if wait:
                    dve.wait_ge(vec_step, base[0] + steps[0])

            def part(start, count, f):
                base[0], steps[0] = start, 0
                f()
                assert steps[0] == count, (steps[0], count)

            def residual(uses, k, t, n):
                dve.wait_ge(wide_full, uses.full(k))
                link_taken(dve, dve.tensor_tensor(acc[:, t, half(n)], bank(k), acc[:, t, half(n)], ALU.add), uses, k)

            def start():
                def low_x(ns):
                    for n in ns:
                        k = USE_X[n]
                        dve.wait_ge(xt_hi, n + 1)
                        link_taken(dve, dve.tensor_tensor(x_part(x_lo, n), by_feature_tile(k),
                                                          x_part(x_hi, n).bitcast(F32), ALU.subtract),
                                   START, k)

                low_x(range(4))
                dve.wait_ge(gw_hi, 1)
                link(dve, dve.tensor_tensor(g_lo, g_raw, g_hi.bitcast(F32), ALU.subtract), gw_lo, 1)
                low_x(range(4, KT))
                dve.wait_ge(wide_full, USE_PAR[1] + 1)
                link_taken(dve, dve.tensor_copy(cols[:, 0:P], bank(USE_PAR[0])[:, 0:P]), START, USE_PAR[0])
                link_taken(dve, dve.tensor_copy(cols[:, P:COLS], bank(USE_PAR[1])[:, 0:COLS - P]), START, USE_PAR[1])
                low_x(range(KT, 2 * KT))
                for a, b, f in ((COL_W, COL_G, 0.5), (COL_G, COL_SKIP, 0.25), (COL_SKIP, COL_SCALE, 0.5),
                                (COL_SCALE, COL_LNG, 0.5)):
                    step(dve.tensor_scalar(cols[:, a:b], cols[:, a:b], f, None, ALU.mult))
                dve.wait_ge(const_set, CONST_SETS)
                dve.wait_ge(gate_act, ACT_LN)
                n = 0

                def gate(ins):
                    nonlocal n
                    n += 1
                    link(dve, ins, gate_vec, n)

                gate(dve.scalar_tensor_tensor(out=lf_row, in0=f_row, scalar=0.0, in1=f_abs,
                                              op0=ALU.min, op1=ALU.subtract))
                gate(dve.tensor_tensor_scan(bcum, keep, lf_row, 0.0, ALU.mult, ALU.add))
                gate(dve.tensor_tensor(rows[HI, :], i_row, bcum, ALU.subtract))
                gate(dve.tensor_copy(by_chunk(carry)[:, 1:NC, 0], by_chunk(bcum)[:, 0:NC - 1, CHUNK - 1]))
                gate(dve.tensor_tensor_scan(m_row, carry, rows[HI, :], 0.0, ALU.add, ALU.max))
                assert n == VEC_M
                gate(dve.tensor_tensor(m_prev[:, 1:NC], by_chunk(m_row)[:, 0:NC - 1, CHUNK - 1],
                                       by_chunk(bcum)[:, 0:NC - 1, CHUNK - 1], ALU.add))
                gate(dve.tensor_scalar(m_last, by_chunk(m_row)[:, :, CHUNK - 1], -1.0, None, ALU.mult))
                assert n == VEC_PREV
                gate(dve.tensor_tensor(lf_row, bcum, m_row, ALU.add))
                assert n == VEC_ROWS
            part(0, VEC_START, start)

            def gated_output(h, uses, at, ms=range(4)):
                def summed(m):
                    k, j, n = at[m], m % 2, m // 2
                    dve.wait_ge(wide_full, uses.full(k))
                    link_taken(dve, dve.scalar_tensor_tensor(
                        out=tmp_c[:, half(m % 2)], in0=bank(k), scalar=col(h * 2 + (COL_G + j)),
                        in1=e_buf[:, j, half(n)], op0=ALU.mult, op1=ALU.mult), uses, k)
                    link(dve, dve.tensor_tensor(tmp_c[:, half(m % 2)], tmp_c[:, half(m % 2)],
                                                f_buf[:, j, half(n)], ALU.add), y_sum, h * 4 + (m + 1))

                for m in range(ms[0], ms[-1] + 2):
                    if m in ms:
                        summed(m)
                    if m - 1 in ms:
                        lo_part(h * 4 + m, m - 1, tmp_c[:, half((m - 1) % 2)])

            def lo_part(n, m, src):
                dve.wait_ge(y_rounded, n)
                dst = (slice(None), m % 2, half(m // 2))
                link(dve, dve.tensor_tensor(y_lo[dst], src, y_hi[dst].bitcast(F32), ALU.subtract), y_ready, n)

            def head(h, at, first, last=False):
                uses = head_uses(h)

                def conv(j):
                    def tap(i):
                        if i == 0:
                            for n in range(2):
                                wait_taken(dve, uses, at["xm"][j] + n)
                            step(dve.tensor_scalar(tmp_a[:, :], xm[:, j, HALO:HALO + S],
                                                   col(h * 2 + (COL_W + 3 * ET + j)), col(h * 2 + (COL_B + j)),
                                                   ALU.mult, ALU.add))
                            return
                        w = HALO - i
                        ins = dve.scalar_tensor_tensor(
                            out=tmp_a[:, :], in0=xm[:, j, w:w + S], scalar=col(h * 2 + (COL_W + w * ET + j)),
                            in1=tmp_a[:, :], op0=ALU.mult, op1=ALU.add)
                        if i < HALO:
                            step(ins)
                        else:
                            link(dve, ins, conv_ready, h * 2 + (j + 1))

                    def gate():
                        dve.wait_ge(conv_tanh, h * 2 + (j + 1))
                        link(dve, dve.scalar_tensor_tensor(out=xc[:, j, :], in0=tmp_c[:, :], scalar=1.0,
                                                           in1=tmp_a[:, :], op0=ALU.add, op1=ALU.mult),
                             xc_ready, h * 2 + (j + 1))
                    return [lambda i=i: tap(i) for i in range(CONV)] + [gate]

                work = conv(0) + conv(1)
                if first:
                    for f in work:
                        f()
                else:
                    gated_output(h - 1, uses, [at["hn"] + m for m in range(4)])
                    for n in range(2):
                        for t in range(NC):
                            residual(uses, at["out"] + n * NC + t, t, n)
                            if t % 2 and len(work) > 2:
                                work.pop(0)()
                    for f in work:
                        f()
                def low_xm(n):
                    dve.wait_ge(xm_high, h * 2 + (n + 1))
                    link(dve, dve.tensor_tensor(xm_lo[:, :, :], xm[:, :, HALO + n * HALF:HALO + (n + 1) * HALF],
                                                xm_hi[:, :, :].bitcast(F32), ALU.subtract),
                         xm_low, h * 2 + (n + 1))

                for m in range(4):
                    k, j, n = at["z"] + m, m // 2, m % 2
                    dve.wait_ge(z_tanh, h * 4 + (m + 1))
                    link_taken(dve, dve.scalar_tensor_tensor(
                        out=e_buf[:, j, half(n)], in0=gate_t[:, m % 2, :], scalar=1.0, in1=bank(k),
                        op0=ALU.add, op1=ALU.mult), uses, k)
                    if n:
                        step(dve.tensor_tensor(f_buf[:, j, :], f_buf[:, j, :], e_buf[:, j, :], ALU.mult))
                    else:
                        step(dve.tensor_scalar(f_buf[:, j, :], xc[:, j, :], col(h * 2 + (COL_SKIP + j)), None, ALU.mult))
                        dve.wait_ge(xc_high, h * 2 + (j + 1))
                        link(dve, dve.tensor_tensor(xc_lo[:, j, :], xc[:, j, :], xc_hi[:, j, :].bitcast(F32),
                                                    ALU.subtract), xc_low, h * 2 + (j + 1))
                    if m == 2:
                        low_xm(0)
                low_xm(1)

                def gate_col(c, q):
                    return gcol[:, c, q, bass.ds(h, 1)]

                def distance(c):
                    link(dve, dve.scalar_tensor_tensor(out=dist[:, :], in0=m_bc[:, tile(c)], scalar=gate_col(c, 0),
                                                       in1=mask[:, :], op0=ALU.subtract, op1=ALU.add),
                         dist_ready, h * NC + (c + 1))

                def weighted(c):
                    dve.wait_ge(s_full, h * NC + (c + 1))
                    dve.wait_ge(wgt_ready, h * NC + (c + 1))
                    ins = dve.tensor_tensor(sT[:, :], ps_s[:, 0:P], wgt[:, :], ALU.mult)
                    if c == NC - 1:
                        link(dve, ins, s_taken, h * NC + (c + 1))
                        return
                    step(ins)
                    link(dve, dve.tensor_scalar(kw[:, :], ps_s[:, P:2 * P], gate_col(c, 3), None, ALU.mult),
                         s_taken, h * NC + (c + 1))

                def scales(f):
                    part = slice(4 * f, 4 * f + 4)
                    big, r, r2, var = (small[:, i, part] for i in range(4))
                    step(dve.scalar_tensor_tensor(out=big, in0=num[:, part, DV], scalar=-1.0,
                                                  in1=gcol[:, part, 2, bass.ds(h, 1)].rearrange("p c o -> p (c o)"),
                                                  op0=ALU.mult, op1=ALU.max), wait=False)
                    for c in range(4 * f, 4 * f + 4):
                        step(dve.bn_aggr(mv[:, c, :], stats[:, c, :]), wait=c == 4 * f + 3)
                    step(dve.tensor_tensor(big, num[:, part, DV], big, ALU.max))
                    step(dve.reciprocal(r, big))
                    step(dve.tensor_tensor(r2, r, r, ALU.mult))
                    step(dve.tensor_tensor(var, r2, mv[:, part, 1], ALU.mult))
                    link(dve, dve.tensor_scalar(var, var, EPS, None, ALU.add), var_ready, h * 2 + (f + 1))

                def norm(f):
                    part = slice(4 * f, 4 * f + 4)
                    dve.wait_ge(rstd_ready, h * 2 + (f + 1))
                    step(dve.tensor_tensor(small[:, 2, part], small[:, 1, part], rstd[:, part], ALU.mult))
                    for c in range(4 * f, 4 * f + 4):
                        ins = dve.tensor_scalar(num[:, c, 0:DV], num[:, c, 0:DV], mv[:, c, 0:1],
                                                small[:, 2, c:c + 1], ALU.subtract, ALU.mult)
                        if c % 4 == 3:
                            link(dve, ins, hn_ready, h * 2 + (f + 1))
                        else:
                            step(ins)

                if first:
                    dve.wait_ge(rows_full, 1)
                    for m, ps in enumerate((ps_intra, ps_inter)):
                        step(dve.tensor_copy(gcol[:, 4 * m:4 * m + 4, :, :],
                                             ps[:, :].rearrange("p (c q r) -> p c q r", c=4, q=4)[:, :, :, 0:HEADS]))
                    dve.wait_ge(wc_in, 16)
                dve.wait_ge(m_in, h * 16 + 16)
                distance(0)
                weighted(0)
                distance(1)
                for c in range(NC):
                    dve.wait_ge(num_full, h * NC + (c + 1))
                    if c == 0:
                        link(dve, dve.tensor_copy(state[:, :], ps_state[:, 0:DV + 1]), state_ready,
                             h * (NC - 1) + (c + 1))
                    elif c < NC - 1:
                        link(dve, dve.scalar_tensor_tensor(out=state[:, :], in0=state[:, :],
                                                           scalar=wc_bc[:, bass.ds(h * NC + c, 1)],
                                                           in1=ps_state[:, 0:DV + 1], op0=ALU.mult, op1=ALU.add),
                             state_ready, h * (NC - 1) + (c + 1))
                    dve.wait_ge(intra_taken, h * NC + (c + 1))
                    if c:
                        step(dve.scalar_tensor_tensor(out=num[:, c, :], in0=ps_inter[:, 0:DV + 1],
                                                      scalar=gate_col(c, 1), in1=num[:, c, :],
                                                      op0=ALU.mult, op1=ALU.add))
                    if c + 1 < NC:
                        weighted(c + 1)
                    if c + 2 < NC:
                        distance(c + 2)
                    if first:
                        step(dve.tensor_scalar(acc[:, c, :], acc[:, c, :], ALPHA, None, ALU.mult))
                    if last and c == NC - 1:
                        gated_output(h, BETWEEN, BRIDGE_T, range(2))
                    step(dve.bn_stats(stats[:, c, :], num[:, c, 0:DV]))
                    if c % 2:
                        m = c // 2
                        wait_taken(dve, uses, at["o"] + m)
                        j, n = m // 2, m % 2
                        link(dve, dve.scalar_tensor_tensor(out=e_buf[:, j, half(n)], in0=gate_t[:, m % 2, :],
                                                           scalar=1.0, in1=e_buf[:, j, half(n)],
                                                           op0=ALU.add, op1=ALU.mult), o_used, h * 4 + (m + 1))
                    if c == 4:
                        scales(0)
                    if c == 6:
                        norm(0)
                scales(1)
                norm(1)

            part(VEC_START, VEC_FIRST, lambda: head(0, FIRST, True))
            with dve.Fori(1, HEADS - 1) as h:
                part(h * VEC_LATER + (VEC_START + VEC_FIRST - VEC_LATER), VEC_LATER, lambda: head(h, LATER, False))
            part(VEC_START + VEC_FIRST + (HEADS - 2) * VEC_LATER, VEC_LATER,
                 lambda: head(HEADS - 1, LATER, False, True))

            def residual_sum(uses, k, t, n):
                dve.wait_ge(wide_full, uses.full(k))
                link_taken(dve, dve.scalar_tensor_tensor(out=acc[:, t, half(n)], in0=bank(k), scalar=1.0,
                                                         in1=acc[:, t, half(n)], op0=ALU.mult, op1=ALU.add,
                                                         accum_out=small[:, n, t:t + 1]), uses, k)

            def mean(t, n):
                link(dve, dve.tensor_scalar(small[:, 2, t:t + 1], small[:, 0, t:t + 1], small[:, 1, t:t + 1],
                                            -1.0 / D, ALU.add, ALU.mult), ln_mean, n + t + 1)

            def between():
                def residual_out(i):
                    t, n = TAIL_OUT[i]
                    residual_sum(BETWEEN, BRIDGE_O[i], t, n)
                    if n:
                        mean(t, 0)

                def norm_tile(t):
                    dve.wait_ge(ln_rstd, t + 1)
                    link(dve, dve.tensor_scalar(acc[:, t, :], acc[:, t, :], small[:, 2, t:t + 1],
                                                rstd[:, t:t + 1], ALU.add, ALU.mult), ln_x, t + 1)

                def form_x(n):
                    t = n % KT
                    if n >= 4 and n % 2 == 0:
                        dve.wait_ge(x1_lo[0], (n - 4) // 2 + 1)
                    dve.wait_ge(x1_full, n + 1)
                    link(dve, dve.tensor_scalar(x_new[:, n % 4, :], x_bank(n), cols[:, COL_LNG + t:COL_LNG + t + 1],
                                                cols[:, COL_LNB + t:COL_LNB + t + 1], ALU.mult, ALU.add),
                         x1_taken[1], formed(n)[1])

                def low_odd(n):
                    dve.wait_ge(x1_hi, n + 1)
                    dst = (slice(None), n % KT, half(n // KT))
                    link(dve, dve.tensor_tensor(x_lo[dst], x_new[:, n % 4, :], x_hi[dst].bitcast(F32),
                                                ALU.subtract), x1_lo[1], n // 2 + 1)

                for t in range(6):
                    residual_out(2 * t)
                    residual_out(2 * t + 1)
                    if t:
                        norm_tile(t - 1)
                    if t == 1:
                        gated_output(HEADS - 1, BETWEEN, BRIDGE_T, range(2, 4))
                form_x(1)
                form_x(2)
                residual_out(12)
                low_odd(1)
                norm_tile(5)
                form_x(3)
                residual_out(13)
                low_odd(3)
                residual_out(14)
                residual_out(15)
                form_x(5)
                form_x(6)
                low_odd(5)
                form_x(7)
                low_odd(7)
                norm_tile(6)
                norm_tile(7)
                for n in (9, 13):
                    form_x(n)
                    form_x(n + 1)
                    low_odd(n)
                    form_x(n + 2)
                    low_odd(n + 2)
                dve.wait_ge(gb_in, 32)
                for v in (g_first, b_first[:, :]):
                    step(dve.tensor_scalar(v, v, ALPHA, None, ALU.mult))
                dve.wait_ge(pool_set, POOL_SETS)

            at_pool = VEC_START + VEC_FIRST + (HEADS - 1) * VEC_LATER
            part(at_pool, VEC_BETWEEN, between)

            def group(g, first, last):
                uses = group_uses(g)

                def gain(t):
                    link(dve, dve.tensor_tensor(acc[:, t, :], acc[:, t, :], g_first, ALU.mult), acc_gain, t + 1)

                for j in range(4):
                    if first and j < 2:
                        wait_taken(dve, uses, 2 + j)
                    else:
                        for n in range(2):
                            wait_taken(dve, uses, G_U + 2 * j + n)
                    src = u_buf[:, j % 2, :]
                    for level, dst in enumerate((win_a, win_b, win_a, win_b)):
                        back = PAD - (1 << level)
                        step(dve.scalar_tensor_tensor(out=dst[:, PAD:PAD + S], in0=src[:, back:back + S],
                                                      scalar=flag[:, bass.ds(g * GROUPS + level, 1)],
                                                      in1=src[:, PAD:PAD + S], op0=ALU.mult, op1=ALU.add))
                        src = dst
                    step(dve.tensor_tensor(win_b[:, PAD:2 * PAD], win_b[:, PAD:2 * PAD],
                                           head_fix[:, bass.ds(g * PAD, PAD)], ALU.mult))
                    link(dve, dve.scalar_tensor_tensor(out=win_a[:, PAD:PAD + S], in0=win_b[:, PAD:PAD + S],
                                                       scalar=inv_win[:, bass.ds(g, 1)],
                                                       in1=u_buf[:, j % 2, PAD:PAD + S],
                                                       op0=ALU.mult, op1=ALU.subtract), pool_sum, g * 4 + (j + 1))
                    dve.wait_ge(pool_rounded, g * 4 + (j + 1))
                    link(dve, dve.tensor_tensor(p_lo[:, j, :], win_a[:, PAD:PAD + S], p_hi[:, j, :].bitcast(F32),
                                                ALU.subtract), pool_ready, g * 4 + (j + 1))
                    if first and j < 2:
                        gain(j)

                def z_gate(p):
                    for m in range(4):
                        k = G_Z[p] + m
                        dve.wait_ge(z_tanh, g * 8 + (4 * HEADS + 4 * p + m + 1))
                        link_taken(dve, dve.scalar_tensor_tensor(
                            out=zz[:, m // 2, half(m % 2)], in0=gate_t[:, m % 2, :], scalar=1.0, in1=bank(k),
                            op0=ALU.add, op1=ALU.mult), uses, k)
                        if first and p == 0:
                            for t in ((2, 3), (4, 5), (6,), (7,))[m]:
                                gain(t)

                def mixed(p):
                    for m in range(5):
                        if m < 4:
                            k = G_MIX[p] + m
                            dve.wait_ge(wide_full, uses.full(k))
                            link_taken(dve, dve.scalar_tensor_tensor(
                                out=y_t[:, m % 2, :], in0=bank(k), scalar=col(g * 4 + (COL_SCALE + 2 * p + m % 2)),
                                in1=zz[:, m % 2, half(m // 2)], op0=ALU.mult, op1=ALU.mult), uses, k)
                        if m:
                            lo_part(g * 8 + (4 * HEADS + 4 * p + m), m - 1, y_t[:, (m - 1) % 2, :])

                def project(p):
                    for n in range(2):
                        for t in range(NC):
                            residual(uses, G_OUT[p] + n * NC + t, t, n)

                z_gate(0)
                mixed(0)
                z_gate(1)
                if first:
                    dve.wait_ge(acc_ready, NC)
                project(0)
                mixed(1)
                if not last:
                    project(1)
                    return
                dve.wait_ge(gb_in, 64)
                for i, (t, n) in enumerate(LAST_PROJECT):
                    residual_sum(uses, G_OUT[1] + i, t, n)
                    if n:
                        mean(t, NC)
                        link(dve, dve.scalar_tensor_tensor(out=normed[t], in0=acc[:, t, :], scalar=small[:, 2, t:t + 1],
                                                           in1=g_bc[:, :], op0=ALU.add, op1=ALU.mult), ln_gain, t + 1)
                for t in range(LATE, NC):
                    dve.wait_ge(ln_rstd, NC + t + 1)
                    for n in range(2):
                        link(dve, dve.scalar_tensor_tensor(out=normed[t][:, half(n)], in0=normed[t][:, half(n)],
                                                           scalar=rstd[:, t:t + 1], in1=b_bc[:, half(n)],
                                                           op0=ALU.mult, op1=ALU.add),
                             ln_done_late, 2 * (t - LATE) + n + 1)

            at_pool += VEC_BETWEEN
            part(at_pool, VEC_GROUP, lambda: group(0, True, False))
            with dve.Fori(1, GROUPS - 1) as g:
                part(g * VEC_GROUP + at_pool, VEC_GROUP, lambda: group(g, False, False))
            part(at_pool + (GROUPS - 1) * VEC_GROUP, VEC_GROUP, lambda: group(GROUPS - 1, False, True))

        @block.tensor
        def _(pe):
            def free(uses, k):
                if uses is not START or k >= 4:
                    pe.wait_ge(wide_taken[k % 4], uses.taken(k - 4))

            def split(dst, a, b, first, last):
                pe.matmul(dst, a[0], b[0], start=first, stop=False)
                pe.matmul(dst, a[0], b[1], start=False, stop=False)
                return pe.matmul(dst, a[1], b[0], start=False, stop=last)

            def in_product(uses, k, n, w, between=None, ready=None):
                free(uses, k)
                for t in range(KT):
                    if ready:
                        ready(t)
                    mm = split(bank(k), [v[:, tile(t)] for v in w], [v[:, t, half(n)] for v in (x_hi, x_lo)],
                               t == 0, t == KT - 1)
                    if t == KT - 1:
                        mm.then_inc(wide_full, 1)
                    if between:
                        between(t)

            def slot(s0, k):
                pe.wait_ge(lo_ready, s0 + (k + 1))
                return w_hi[:, k % 2, :], w_lo[:, k % 2, :]

            def in_slot(uses, s0, ks, k, between=None):
                w = slot(s0, ks)
                for n in range(2):
                    in_product(uses, k + n, n, w, between)

            def out_product(uses, k, w, t, y_before=None):
                free(uses, k)
                for j in range(2):
                    if y_before is not None and t % 4 == 0:
                        pe.wait_ge(y_ready, y_before + (1 + t // 2 + j))
                    mm = split(bank(k), [v[:, j, tile(t)] for v in (y_hi, y_lo)],
                               [v[:, half(j)] for v in w], j == 0, j == 1)
                mm.then_inc(wide_full, 1)

            def project(uses, k, s0, ks, y_before):
                for n in range(2):
                    w = slot(s0, ks + n)
                    for t in range(NC):
                        out_product(uses, k + n * NC + t, w, t, None if n else y_before)

            def project_by_token(uses, k, s0, ks, y_before):
                ws = {}
                for i, (t, n) in enumerate(LAST_PROJECT):
                    if n not in ws:
                        ws[n] = slot(s0, ks + n)
                    out_product(uses, k + i, ws[n], t, None if n else y_before)

            def turn(uses, k, srcs):
                free(uses, k)
                for i, src in enumerate(srcs):
                    mm = pe.transpose(bank(k)[:, tile(i)], src, ident[:, :])
                mm.then_inc(wide_full, 1)

            def x_turns(m):
                for n in range(KT * m, KT * m + KT):
                    t, f = n // 2, n % 2
                    if f == 0:
                        pe.wait_ge(x_in[t], 16)
                    turn(START, USE_X[n], [acc[:, t, tile(4 * f + i)] for i in range(4)])

            def x_ready(m):
                def wait(t):
                    if t % 4 == 0:
                        for i in range(4):
                            wait_taken(pe, START, USE_X[KT * m + 2 * i + t // 4])
                return wait

            pe.wait_ge(const_set, SET_IDENT)
            x_turns(0)
            pe.wait_ge(gw_lo, 1)
            in_product(START, USE_GATES[0], 0, (g_hi, g_lo), ready=x_ready(0))
            pe.wait_ge(par_in, 16 * 7)
            for b in range(2):
                turn(START, USE_PAR[b], [par_rows[:, b, :]])
            x_turns(1)
            in_product(START, USE_GATES[1], 1, (g_hi, g_lo), ready=x_ready(1))

            def turn_hn(h, uses, at, ms=range(4)):
                for m in ms:
                    if m % 2 == 0:
                        pe.wait_ge(hn_ready, h * 2 + (m // 2 + 1))
                    turn(uses, at[m], [num[:, 4 * (m // 2) + i, (m % 2) * P:(m % 2 + 1) * P] for i in range(4)])

            def head(h, at, first):
                uses, s0 = head_uses(h), slot_base(h)
                in_slot(uses, s0, 0, at["xm"][0])
                if not first:
                    turn_hn(h - 1, uses, [at["hn"] + m for m in range(4)])
                in_slot(uses, s0, 1, at["xm"][1])
                if not first:
                    project(uses, at["out"], s0, at["s_out"], h * 4 - 4)
                for j in range(2):
                    in_slot(uses, s0, at["s_z"] + j, at["z"] + 2 * j)
                if first:
                    pe.wait_ge(gate_act, ACT_ROWS)
                    for c in range(NC):
                        mm = pe.transpose((ps_intra, ps_inter)[c // 4][:, tile(c % 4)], rows[:, tile(c)], ident[:, :])
                    mm.then_inc(rows_full, 1)
                def query_or_key(k, w):
                    for n in range(2):
                        free(uses, k + n)
                        for j in range(2):
                            if w == 0 and n == 0:
                                pe.wait_ge(xc_low, h * 2 + (j + 1))
                            at_w = slice(w + j * DK, w + (j + 1) * DK)
                            mm = split(bank(k + n), [v[:, at_w] for v in (qkv_hi, qkv_lo)],
                                       [v[:, j, half(n)] for v in (xc_hi, xc_lo)], j == 0, j == 1)
                        mm.then_inc(wide_full, 1)

                def values(m):
                    pe.wait_ge(xm_low, h * 2 + (m + 1))
                    for k in at["v"][2 * m:2 * m + 2]:
                        free(uses, k)
                        for i in range(2):
                            t = 2 * (at["v"].index(k) % 2) + i
                            for j in range(2):
                                w = 4 * DK + j * DV
                                mm = split(bank(k)[:, i * DV:(i + 1) * DV], [v[:, j, tile(t)] for v in (xm_hi, xm_lo)],
                                           [v[:, w:w + DV] for v in (qkv_hi, qkv_lo)], j == 0, j == 1)
                        mm.then_inc(wide_full, 1)

                pe.wait_ge(qkv_low, h + 1)
                query_or_key(at["q"], 0)
                values(0)
                query_or_key(at["k"], 2 * DK)
                values(1)

                def scores(c):
                    if c < NC - 1:
                        pe.transpose(ps_s[:, P:2 * P], kT[:, tile(c)], ident[:, :])
                    pe.matmul(ps_s[:, 0:P], kT[:, tile(c)], qT[:, tile(c)], start=True, stop=True).then_inc(s_full, 1)

                def outputs(c):
                    if c == 0:
                        for n in range(4):
                            wait_taken(pe, uses, at["v"][n])
                    pe.wait_ge(s_taken, h * NC + (c + 1))
                    mm = pe.matmul(ps_intra[:, 0:DV + 1], sT[:, :], v_sb[:, c, :], start=True, stop=True)
                    if c:
                        pe.wait_ge(state_ready, h * (NC - 1) + c)
                        mm = pe.matmul(ps_inter[:, 0:DV + 1], qT[:, tile(c)], state[:, :], start=True, stop=True)
                    if c < NC - 1:
                        mm = pe.matmul(ps_state[:, 0:DV + 1], kw[:, :], v_sb[:, c, :], start=True, stop=True)
                    mm.then_inc(num_full, 1)

                for n in range(2):
                    wait_taken(pe, uses, at["k"] + n)
                scores(0)
                chunk = [0]

                def core(t):
                    if t % 4 != 3:
                        return
                    c = chunk[0]
                    outputs(c)
                    if c + 1 < NC:
                        scores(c + 1)
                    chunk[0] += 1

                for j in range(2):
                    in_slot(uses, s0, at["s_o"] + j, at["o"] + 2 * j, core)

            head(0, FIRST, True)
            with pe.Fori(1, HEADS) as h:
                head(h, LATER, False)
            def turn_x(n):
                m, t = n // KT, n % KT
                if t == 0:
                    pe.wait_ge(ln_x, 4 * m + 4)
                if n >= 4:
                    by, count = formed(n - 4)
                    pe.wait_ge(x1_taken[by], count)
                for i in range(4):
                    mm = pe.transpose(x_bank(n)[:, tile(i)], acc[:, 4 * m + i, tile(t)], ident[:, :])
                mm.then_inc(x1_full, 1)

            def input_ready(m):
                return lambda t: pe.wait_ge(x1_lo[t % 2], KT // 2 * m + t // 2 + 1)

            ws = []
            for kind, i in BRIDGE:
                k = BRIDGE_WIDE.index((kind, i)) if kind != "X" else None
                if kind == "T":
                    turn_hn(HEADS - 1, BETWEEN, BRIDGE_T, (i,))
                elif kind == "O":
                    if i < 2:
                        ws.append(slot(SLOT_LAST_OUT, i))
                    t, n = TAIL_OUT[i]
                    out_product(BETWEEN, k, ws[n], t, None if n else 4 * HEADS - 4)
                elif kind == "X":
                    turn_x(i)
                elif kind == "U":
                    def between(t):
                        for n in X_IN_U[i].get(t, ()):
                            turn_x(n)

                    in_product(BETWEEN, k, 0, slot(SLOT_POOL, i), between, None if i else input_ready(0))

            def group(g, first, last):
                uses, s0 = group_uses(g), g * SLOTS_PER_GROUP + SLOT_POOL
                y0 = g * 8 + 4 * HEADS
                if first:
                    for j in range(2):
                        in_product(uses, 2 + j, 1, slot(s0, GS_U + j), ready=None if j else input_ready(1))
                for j in range(2 if first else 0, 4):
                    in_slot(uses, s0, GS_U + j, G_U + 2 * j)

                def z_and_mix(p):
                    for j in range(2):
                        in_slot(uses, s0, GS_Z[p] + j, G_Z[p] + 2 * j)
                    if p:
                        project(uses, G_OUT[0], s0, GS_OUT[0], y0)
                    w = slot(s0, GS_MIX[p])
                    for m in range(4):
                        n, j, k = m // 2, m % 2, G_MIX[p] + m
                        free(uses, k)
                        for t in range(4):
                            if p == 0 and m == 0:
                                pe.wait_ge(pool_ready, g * 4 + (t + 1))
                            at = t * 2 * P + j * P
                            mm = split(bank(k), [v[:, at:at + P] for v in w],
                                       [v[:, t, half(n)] for v in (p_hi, p_lo)], t == 0, t == 3)
                        mm.then_inc(wide_full, 1)

                z_and_mix(0)
                z_and_mix(1)
                (project_by_token if last else project)(uses, G_OUT[1], s0, GS_OUT[1], y0 + 4)

            group(0, True, False)
            with pe.Fori(1, GROUPS - 1) as g:
                group(g, False, False)
            group(GROUPS - 1, False, True)


_INS = ("x", "mlstm_w_in", "mlstm_conv_w", "mlstm_conv_b", "mlstm_w_q", "mlstm_w_k", "mlstm_w_v", "mlstm_b_i",
        "mlstm_b_f", "mlstm_norm_g", "mlstm_skip", "mlstm_w_out", "pool_w_in", "pool_w_group", "pool_scale",
        "pool_w_out", "post_ln_g", "post_ln_b")
_KEEP_LAYER_AXIS = ("mlstm_conv_b", "mlstm_b_i", "mlstm_b_f", "mlstm_norm_g", "mlstm_skip", "pool_scale",
                    "post_ln_g", "post_ln_b")


def kernel(**inputs):
    from concourse import bacc
    from concourse.bass_utils import run_bass_kernel_spmd

    nc = bacc.Bacc("TRN2", target_bir_lowering=False, num_devices=1)
    arrays, args = {}, []
    for name in _INS:
        a = np.ascontiguousarray(inputs[name])
        if name not in _KEEP_LAYER_AXIS:
            a = a[0]
        arrays[f"in_{name}"] = a
        args.append(nc.dram_tensor(f"in_{name}", a.shape, F32, kind="ExternalInput").ap())
    out = nc.dram_tensor("out", (S, D), F32, kind="ExternalOutput").ap()
    build(nc, *args, out)
    got = run_bass_kernel_spmd(nc, [arrays], core_ids=[0])
    return got.results[0]["out"].reshape(1, S, D)
```
